# Optimizing a Trainium2 kernel written in Bass

```python
import jax, jax.numpy as jnp
from jax import lax
import numpy as np

D_MODEL = 1024
BATCH = 1
SEQ = 512
DEPTH = 2

N_A_LAYERS = DEPTH // 2
N_B_LAYERS = DEPTH - N_A_LAYERS

GDN_HEADS = 8
GDN_DK = 128
GDN_DV = 128
D_QK = GDN_HEADS * GDN_DK
D_VA = GDN_HEADS * GDN_DV
GDN_CONV_CH = 2 * D_QK + D_VA
GDN_IN = 2 * D_QK + 2 * D_VA + 2 * GDN_HEADS
CONV_WIDTH = 4
CHUNK = 64
MLA_HEADS = 8
Q_LORA = 512
KV_LORA = 256
D_NOPE = 128
D_ROPE = 64
D_V = 128
ROPE_THETA = 10000.0
Q_BLOCK = 128
N_EXPERTS = 64
TOP_K = 8
N_GROUPS = 8
TOPK_GROUPS = 4
D_EXPERT = 256
D_SHARED = 256
ROUTED_SCALE = 2.5
EXPERT_BLOCK = 128
DN_ALPHA = (2 * DEPTH) ** 0.25
DN_BETA = (8 * DEPTH) ** -0.25
EPS = 1e-6
LN_EPS = 1e-5
F32 = jnp.float32

kernel_name = 'yoco_gdn_mla_moe_deepnorm'

def layer_norm(x, g, b):
    xf = x.astype(F32)
    mu = jnp.mean(xf, -1, keepdims=True)
    var = jnp.mean(jnp.square(xf - mu), -1, keepdims=True)
    return ((xf - mu) * lax.rsqrt(var + LN_EPS) * g + b).astype(x.dtype)

def rms_norm(x, w):
    xf = x.astype(F32)
    return (xf * lax.rsqrt(jnp.mean(xf * xf, -1, keepdims=True) + EPS) * w).astype(x.dtype)

def l2_norm(x):
    return x * lax.rsqrt(jnp.sum(x * x, -1, keepdims=True) + EPS)

def rope_tables(L):
    inv = 1.0 / (ROPE_THETA ** (jnp.arange(0, D_ROPE, 2, dtype=F32) / D_ROPE))
    ang = jnp.arange(L, dtype=F32)[:, None] * inv[None, :]
    return jnp.cos(ang), jnp.sin(ang)

def apply_rope(x, cos, sin):
    x1, x2 = jnp.split(x.astype(F32), 2, axis=-1)
    return jnp.concatenate([x1 * cos - x2 * sin, x2 * cos + x1 * sin], -1).astype(x.dtype)

def causal_dwconv_silu(x, w):
    C = x.shape[-1]
    y = lax.conv_general_dilated(x, w[:, None, :].astype(x.dtype), window_strides=(1,),
                                 padding=[(CONV_WIDTH - 1, 0)],
                                 dimension_numbers=('NWC', 'WIO', 'NWC'),
                                 feature_group_count=C)
    return jax.nn.silu(y)

def chunk_gated_delta_rule(q, k, v, g, beta):
    B, L, H, DK = q.shape
    DV = v.shape[-1]
    N = L // CHUNK

    def chunks(t):
        t = t.reshape((B, N, CHUNK, H) + t.shape[3:])
        return jnp.moveaxis(t, (1, 3), (0, 2))

    q, k, v, g, beta = (chunks(t) for t in (q, k, v, g, beta))
    g = jnp.cumsum(g, axis=-1)
    pos = jnp.arange(CHUNK)
    incl = pos[:, None] >= pos[None, :]
    strict = pos[:, None] > pos[None, :]
    decay = jnp.exp(jnp.where(incl, g[..., :, None] - g[..., None, :], -jnp.inf))
    kb = k * beta[..., None]
    lower = jnp.where(strict, jnp.einsum('nbhid,nbhjd->nbhij', kb, k) * decay, 0.0)
    rhs = jnp.concatenate([v * beta[..., None], kb * jnp.exp(g)[..., None]], -1)
    sol = lax.linalg.triangular_solve(jnp.eye(CHUNK, dtype=F32) + lower, rhs,
                                      left_side=True, lower=True, unit_diagonal=True)
    u, w = sol[..., :DV], sol[..., DV:]
    attn = jnp.einsum('nbhid,nbhjd->nbhij', q, k) * decay

    def step(S, inp):
        qc, kc, uc, wc, gc, ac = inp
        v_new = uc - jnp.einsum('bhck,bhkv->bhcv', wc, S)
        o = (jnp.einsum('bhck,bhkv->bhcv', qc * jnp.exp(gc)[..., None], S)
             + jnp.einsum('bhij,bhjv->bhiv', ac, v_new))
        g_last = gc[..., -1:]
        S = (S * jnp.exp(g_last)[..., None]
             + jnp.einsum('bhck,bhcv->bhkv', kc * jnp.exp(g_last - gc)[..., None], v_new))
        return S, o

    S0 = jnp.zeros((B, H, DK, DV), F32)
    _, o = lax.scan(step, S0, (q, k, u, w, g, attn))
    return jnp.moveaxis(o, (0, 2), (1, 3)).reshape(B, L, H, DV)

def gated_deltanet(x, w_in, conv_w, A_log, dt_bias, onorm_w, w_out):
    B, L, _ = x.shape
    H = GDN_HEADS
    proj = x @ w_in
    qkv, z, a, b = jnp.split(proj, [GDN_CONV_CH, GDN_CONV_CH + D_VA, GDN_CONV_CH + D_VA + H], axis=-1)
    qkv = causal_dwconv_silu(qkv, conv_w)
    q, k, v = jnp.split(qkv, [D_QK, 2 * D_QK], axis=-1)
    q = l2_norm(q.reshape(B, L, H, GDN_DK).astype(F32)) * (GDN_DK ** -0.5)
    k = l2_norm(k.reshape(B, L, H, GDN_DK).astype(F32))
    v = v.reshape(B, L, H, GDN_DV).astype(F32)
    beta = jax.nn.sigmoid(b.astype(F32))
    g = -jnp.exp(A_log.astype(F32)) * jax.nn.softplus(a.astype(F32) + dt_bias.astype(F32))
    o = chunk_gated_delta_rule(q, k, v, g, beta)
    o = rms_norm(o, onorm_w) * jax.nn.silu(z.reshape(B, L, H, GDN_DV).astype(F32))
    return o.reshape(B, L, D_VA).astype(x.dtype) @ w_out

def shared_mla_kv(h, w_dkv, kv_norm_w, w_ukv, cos, sin):
    B, L, _ = h.shape
    ckv = h @ w_dkv
    c = rms_norm(ckv[..., :KV_LORA], kv_norm_w)
    k_rope = apply_rope(ckv[..., KV_LORA:], cos, sin)
    kv = (c @ w_ukv).reshape(B, L, MLA_HEADS, D_NOPE + D_V)
    return kv[..., :D_NOPE], k_rope, kv[..., D_NOPE:]

def mla_attention(x, w_dq, qnorm_w, w_uq, w_o, k_nope, k_rope, v, cos, sin):
    B, L, _ = x.shape
    q = (rms_norm(x @ w_dq, qnorm_w) @ w_uq).reshape(B, L, MLA_HEADS, D_NOPE + D_ROPE)
    q_nope = q[..., :D_NOPE]
    q_rope = apply_rope(q[..., D_NOPE:], cos[:, None], sin[:, None])
    nb = L // Q_BLOCK
    scale = (D_NOPE + D_ROPE) ** -0.5
    kpos = jnp.arange(L)

    def blocks(t):
        return jnp.moveaxis(t.reshape((B, nb, Q_BLOCK) + t.shape[2:]), 1, 0)

    def attend(args):
        qn, qr, i = args
        s = (jnp.einsum('bqhd,bkhd->bhqk', qn, k_nope)
             + jnp.einsum('bqhd,bkd->bhqk', qr, k_rope)).astype(F32) * scale
        qpos = i * Q_BLOCK + jnp.arange(Q_BLOCK)
        s = jnp.where(kpos[None, :] <= qpos[:, None], s, -jnp.inf)
        p = jax.nn.softmax(s, axis=-1).astype(v.dtype)
        return jnp.einsum('bhqk,bkhd->bqhd', p, v)

    o = lax.map(attend, (blocks(q_nope), blocks(q_rope), jnp.arange(nb)))
    return jnp.moveaxis(o, 0, 1).reshape(B, L, MLA_HEADS * D_V) @ w_o

def swiglu(x, wg, wu, wd):
    return (jax.nn.silu(x @ wg) * (x @ wu)) @ wd

def route(xf, w_router, bias):
    T = xf.shape[0]
    scores = jax.nn.sigmoid((xf @ w_router).astype(F32))
    biased = scores + bias.astype(F32)
    grouped = biased.reshape(T, N_GROUPS, N_EXPERTS // N_GROUPS)
    group_score = lax.top_k(grouped, 2)[0].sum(-1)
    _, top_groups = lax.top_k(group_score, TOPK_GROUPS)
    group_mask = jax.nn.one_hot(top_groups, N_GROUPS, dtype=F32).sum(1) > 0
    expert_mask = jnp.repeat(group_mask, N_EXPERTS // N_GROUPS, axis=-1)
    _, idx = lax.top_k(jnp.where(expert_mask, biased, -jnp.inf), TOP_K)
    w = jnp.take_along_axis(scores, idx, axis=-1)
    w = w / (w.sum(-1, keepdims=True) + 1e-20) * ROUTED_SCALE
    return idx, w

def routed_experts(xf, idx, w, w_gate, w_up, w_down):
    T, D = xf.shape
    A = T * TOP_K
    n_blocks = -(-A // EXPERT_BLOCK) + N_EXPERTS
    flat_e = idx.reshape(A)
    order = jnp.argsort(flat_e)
    e_sorted = flat_e[order]
    counts = jnp.bincount(flat_e, length=N_EXPERTS)
    padded = (counts + EXPERT_BLOCK - 1) // EXPERT_BLOCK * EXPERT_BLOCK
    pad_end = jnp.cumsum(padded)
    pad_start = pad_end - padded
    start = jnp.cumsum(counts) - counts
    dest = pad_start[e_sorted] + jnp.arange(A) - start[e_sorted]
    slot_tok = jnp.full((n_blocks * EXPERT_BLOCK,), T, jnp.int32).at[dest].set((order // TOP_K).astype(jnp.int32))
    slot_w = jnp.zeros((n_blocks * EXPERT_BLOCK,), F32).at[dest].set(w.reshape(A)[order])
    block_e = jnp.minimum(jnp.searchsorted(pad_end, jnp.arange(n_blocks) * EXPERT_BLOCK, side='right'),
                          N_EXPERTS - 1)
    x_pad = jnp.concatenate([xf, jnp.zeros((1, D), xf.dtype)], axis=0)

    def step(acc, inp):
        tok, wt, e = inp
        y = swiglu(x_pad[tok], w_gate[e], w_up[e], w_down[e]).astype(F32) * wt[:, None]
        return acc.at[tok].add(y), None

    acc, _ = lax.scan(step, jnp.zeros((T + 1, D), F32),
                      (slot_tok.reshape(n_blocks, EXPERT_BLOCK), slot_w.reshape(n_blocks, EXPERT_BLOCK), block_e))
    return acc[:T]

def moe_ffn(x, w_router, router_bias, w_gate, w_up, w_down, ws_gate, ws_up, ws_down):
    B, L, D = x.shape
    xf = x.reshape(B * L, D)
    idx, w = route(xf, w_router, router_bias)
    y = routed_experts(xf, idx, w, w_gate, w_up, w_down) + swiglu(xf, ws_gate, ws_up, ws_down).astype(F32)
    return y.astype(x.dtype).reshape(B, L, D)

def setup_inputs(seed: int = 0) -> dict:
    key = jax.random.key(seed)
    keys = iter(jax.random.split(key, 40))
    D = D_MODEL
    NA, NB = N_A_LAYERS, N_B_LAYERS

    def nrm(shape, scale):
        return jax.random.normal(next(keys), shape, F32) * scale

    def gain(shape):
        return 1.0 + nrm(shape, 0.02)

    a_col_scale = jnp.concatenate([jnp.ones((2 * D_QK,), F32), jnp.full((D_VA,), DN_BETA, F32),
                                   jnp.ones((D_VA + 2 * GDN_HEADS,), F32)])
    dt = jnp.exp(jax.random.uniform(next(keys), (NA, GDN_HEADS), F32,
                                    minval=float(np.log(1e-3)), maxval=float(np.log(1e-1))))
    ukv_col_scale = jnp.tile(jnp.concatenate([jnp.ones((D_NOPE,), F32), jnp.full((D_V,), DN_BETA, F32)]), MLA_HEADS)
    return {
        'x': jax.random.normal(next(keys), (BATCH, SEQ, D), F32),
        'a_w_in': nrm((NA, D, GDN_IN), D ** -0.5) * a_col_scale,
        'a_conv_w': nrm((NA, CONV_WIDTH, GDN_CONV_CH), CONV_WIDTH ** -0.5),
        'a_A_log': jnp.log(jax.random.uniform(next(keys), (NA, GDN_HEADS), F32, minval=1.0, maxval=16.0)),
        'a_dt_bias': dt + jnp.log(-jnp.expm1(-dt)),
        'a_onorm_w': gain((NA, GDN_DV)),
        'a_w_out': nrm((NA, D_VA, D), D_VA ** -0.5 * DN_BETA),
        'b_w_dq': nrm((NB, D, Q_LORA), D ** -0.5),
        'b_qnorm_w': gain((NB, Q_LORA)),
        'b_w_uq': nrm((NB, Q_LORA, MLA_HEADS * (D_NOPE + D_ROPE)), Q_LORA ** -0.5),
        'b_w_o': nrm((NB, MLA_HEADS * D_V, D), (MLA_HEADS * D_V) ** -0.5 * DN_BETA),
        'kv_w_dkv': nrm((D, KV_LORA + D_ROPE), D ** -0.5),
        'kv_norm_w': gain((KV_LORA,)),
        'kv_w_ukv': nrm((KV_LORA, MLA_HEADS * (D_NOPE + D_V)), KV_LORA ** -0.5) * ukv_col_scale,
        'ln1_g': gain((DEPTH, D)),
        'ln1_b': nrm((DEPTH, D), 0.02),
        'ln2_g': gain((DEPTH, D)),
        'ln2_b': nrm((DEPTH, D), 0.02),
        'moe_w_router': nrm((DEPTH, D, N_EXPERTS), D ** -0.5),
        'moe_router_bias': nrm((DEPTH, N_EXPERTS), 0.01),
        'moe_w_gate': nrm((DEPTH, N_EXPERTS, D, D_EXPERT), D ** -0.5),
        'moe_w_up': nrm((DEPTH, N_EXPERTS, D, D_EXPERT), D ** -0.5),
        'moe_w_down': nrm((DEPTH, N_EXPERTS, D_EXPERT, D), D_EXPERT ** -0.5 * DN_BETA),
        'moe_ws_gate': nrm((DEPTH, D, D_SHARED), D ** -0.5),
        'moe_ws_up': nrm((DEPTH, D, D_SHARED), D ** -0.5),
        'moe_ws_down': nrm((DEPTH, D_SHARED, D), D_SHARED ** -0.5 * DN_BETA),
    }

def reference(x, a_w_in, a_conv_w, a_A_log, a_dt_bias, a_onorm_w, a_w_out,
              b_w_dq, b_qnorm_w, b_w_uq, b_w_o, kv_w_dkv, kv_norm_w, kv_w_ukv,
              ln1_g, ln1_b, ln2_g, ln2_b, moe_w_router, moe_router_bias,
              moe_w_gate, moe_w_up, moe_w_down, moe_ws_gate, moe_ws_up, moe_ws_down):
    L = x.shape[1]
    cos, sin = rope_tables(L)
    h = x
    k_nope = k_rope = v = None
    for layer in range(DEPTH):
        if layer < N_A_LAYERS:
            i = layer
            mix = gated_deltanet(h, a_w_in[i], a_conv_w[i], a_A_log[i], a_dt_bias[i], a_onorm_w[i], a_w_out[i])
        else:
            i = layer - N_A_LAYERS
            mix = mla_attention(h, b_w_dq[i], b_qnorm_w[i], b_w_uq[i], b_w_o[i], k_nope, k_rope, v, cos, sin)
        h = layer_norm(DN_ALPHA * h + mix, ln1_g[layer], ln1_b[layer])
        ffn = moe_ffn(h, moe_w_router[layer], moe_router_bias[layer], moe_w_gate[layer], moe_w_up[layer],
                      moe_w_down[layer], moe_ws_gate[layer], moe_ws_up[layer], moe_ws_down[layer])
        h = layer_norm(DN_ALPHA * h + ffn, ln2_g[layer], ln2_b[layer])
        if layer == N_A_LAYERS - 1:
            k_nope, k_rope, v = shared_mla_kv(h, kv_w_dkv, kv_norm_w, kv_w_ukv, cos, sin)
    return h


_drawn_inputs = setup_inputs


def setup_inputs(seed=0):
    import zlib

    import numpy as np

    out = dict(_drawn_inputs(seed))
    spreads = {}
    factors = {'b_qnorm_w': 8.0, 'kv_norm_w': 8.0}
    for name, (base, spread) in spreads.items():
        noise = np.random.default_rng([zlib.crc32(name.encode()), seed]).standard_normal(out[name].shape)
        drawn = base * np.exp(spread * noise) if base else spread * noise
        out[name] = __import__('jax').numpy.asarray(drawn.astype(out[name].dtype))
    for name, factor in factors.items():
        out[name] = (out[name] * factor).astype(out[name].dtype)
    return out
```

```python
from contextlib import ExitStack

import numpy as np

import concourse.bass as bass
from concourse import mybir

F32 = mybir.dt.float32
F32R = mybir.dt.float32r
U32 = mybir.dt.uint32
I32 = mybir.dt.int32
ALU = mybir.AluOpType
ACT = mybir.ActivationFunctionType
AX = mybir.AxisListType

P = 128
T = 512
TT = T // P
D = 1024
KD = D // P
H = 8
HG = 4
CHUNK = 64
CONV = 4
N_QKV = 3 * H
Q_LORA = 512
KQ = Q_LORA // P
KV_LORA = 256
KC = KV_LORA // P
D_ROPE = 64
RH = D_ROPE // 2
QH = P + D_ROPE
E = 64
GROUPS = 8
PER = E // GROUPS
TOP_GROUPS = 4
FE = 256
RING = 6
UNIT = 2048
HALF = UNIT // 2
LOADED = 32
CAP = P
ROWS_MOVED = (64, 80, P)
CH_GU = 4
CH_DOWN = 2
CH = 1024
ROUTED_SCALE = 2.5
ALPHA = 4 ** 0.25
EPS = 1e-6
LN_EPS = 1e-5
NEG = -3.0e38
LEVELS = 6
ATT_SCALE = QH ** -0.5

(C_ID, C_CUM, C_INCL, C_AFTER, C_BEFORE, C_ONES, C_IOTA, C_CAUSAL, C_TOK, C_LOW, C_M0, C_MT) = range(12)
N_CONST = C_MT + LEVELS


def constants():
    i, j = np.arange(P)[:, None], np.arange(P)[None, :]
    same = i // CHUNK == j // CHUNK
    c = np.zeros((P, N_CONST, P), np.float32)
    c[:, C_ID] = i == j
    c[:, C_CUM] = same & (i <= j)
    c[:, C_INCL] = same & (i >= j)
    c[:, C_AFTER] = same & (i > j)
    c[:, C_BEFORE] = i < j
    c[:, C_ONES] = 1
    c[:, C_IOTA] = np.where(j < CAP, j, -1.0e6) + 0 * i
    c[:, C_CAUSAL] = np.where(j <= i, 0, NEG)
    c[:, C_TOK, 0:TT] = np.arange(TT)[None, :] * P + i - T
    g = np.arange(GROUPS)
    c[:, C_LOW, 0:GROUPS * GROUPS] = (g[None, :] < g[:, None]).reshape(1, -1)
    for level in range(LEVELS):
        m = (i >> (level + 1) == j >> (level + 1)) & ((i >> level) & 1 == 1) & ((j >> level) & 1 == 0)
        if level == 0:
            c[:, C_M0] = m
        c[:, C_MT + level] = m.T
    inv = (1.0 / (np.float32(10000.0) ** (np.arange(0, D_ROPE, 2, dtype=np.float32) / np.float32(D_ROPE)))).astype(np.float32)
    ang = np.arange(T, dtype=np.float32)[:, None] * inv[None, :]
    rope = np.stack([np.cos(ang), np.sin(ang)]).astype(np.float32)
    rope = rope.reshape(2, TT, P, RH).transpose(2, 0, 1, 3)
    return c.reshape(P, -1), np.ascontiguousarray(rope).reshape(P, -1)


class Count:

    def __init__(self, sem):
        self.sem, self.base = sem, 0


def build(nc, a, out):
    ctx = ExitStack()
    with ctx:
        def sb(name, shape, dt=F32, scope=ctx):
            return scope.enter_context(nc.sbuf_tensor(name, shape, dt))

        def sem(name):
            return Count(ctx.enter_context(nc.semaphore(name)))

        bank = [ctx.enter_context(nc.psum_tensor(f"bank{i}", [P, 512], F32)) for i in range(8)]
        h_rows = nc.dram_tensor("h_rows", (T, D), F32).ap()
        moe_sum = nc.dram_tensor("moe_sum", (T, D), F32).ap()

        const = sb("const", [P, N_CONST, P])
        ring = sb("ring", [P, RING, UNIT])
        resid = sb("resid", [P, TT, D])
        hT = sb("hT", [P, KD, T])
        eps_col = sb("eps_col", [P, 2])
        ident = const[:, C_ID, :]

        def plane(i):
            return const[:, i, :]

        def planes(i, n=HG):
            return const[:, i:i + 1, :].to_broadcast([P, n, P])

        def heads(ap):
            return ap.rearrange("p (h q) -> p h q", q=P)

        slot_loaded = [sem(f"slot_loaded{i}") for i in range(RING)]
        small_in = sem("small_in")
        chains = {}

        def link(eng, name, ins):
            if name not in chains:
                chains[name] = sem(f"{name}_own_write")
            c = chains[name]
            c.base += 1
            ins.then_inc(c.sem, 1)
            eng.wait_ge(c.sem, c.base)

        qkv_ready = sem("qkv_ready")
        qkv_w_hi = sem("qkv_w_hi")
        qkv_w_lo = sem("qkv_w_lo")
        z_ready = sem("z_ready")
        mix_ready = sem("mix_ready")
        router_ready = sem("router_ready")
        gu_ready = sem("gu_ready")
        down_ready = sem("down_ready")
        gu_hi = sem("gu_hi")
        gu_lo = sem("gu_lo")
        down_hi = sem("down_hi")
        down_lo = sem("down_lo")
        cq_ready = sem("cq_ready")
        ukv_ready = sem("ukv_ready")
        uq_ready = sem("uq_ready")

        def rows_kp(w, c0, width):
            return w.rearrange("(k p) c -> p k c", p=P)[:, :, c0:c0 + width]

        def rows_pk(w, c0, width):
            return w.rearrange("(p k) c -> p k c", p=P)[:, :, c0:c0 + width]

        def flat(w):
            return w.rearrange("(p k) c -> p (k c)", p=P)

        units = {}
        n = 0
        for j in range(12):
            units[n] = (rows_pk(a["a_w_in"][0], 256 * j, 256), 256, qkv_w_lo, 4 * j + 4)
            n += 1
        for j in range(4):
            units[n] = (rows_pk(a["a_w_in"][0], 3072 + 256 * j, 256), 256, z_ready, TT * (j + 1))
            n += 1
        UNIT_OUT, UNIT_ROUTER, UNIT_SHARED, UNIT_EXPERT = [0, 0], [0, 0], [0, 0], [0, 0]

        def tail_units(n, layer, w_out):
            UNIT_OUT[layer] = n
            for j in range(4):
                units[n] = (rows_kp(w_out, 256 * j, 256), 256, mix_ready, 4 * (TT - 1) + j + 1 + 4 * TT * layer)
                n += 1
            UNIT_ROUTER[layer] = n
            units[n] = (flat(a["moe_w_router"][layer]), None, router_ready, 1 + layer)
            n += 1
            UNIT_SHARED[layer] = n
            gu_shared = CH_GU * ((TT + E) * layer + TT)
            gu = CH_GU * E * layer
            down = CH_DOWN * (1 + E) * layer + CH_DOWN
            gate, up = flat(a["moe_ws_gate"][layer]), flat(a["moe_ws_up"][layer])
            for j in range(2):
                half = slice(j * HALF, (j + 1) * HALF)
                units[n + j] = ((gate[:, half], up[:, half]), None, gu_ready, gu_shared)
            units[n + 2] = (flat(a["moe_ws_down"][layer]), None, down_lo, down)
            n += 3
            UNIT_EXPERT[layer] = n
            for e in range(E):
                units[n] = (None, None, gu_lo, gu + CH_GU * e + CH_GU // 2)
                units[n + 1] = (None, None, gu_lo, gu + CH_GU * (e + 1))
                units[n + 2] = (None, None, down_lo, down + CH_DOWN * (e + 1))
                n += 3
            return n

        n = tail_units(n, 0, a["a_w_out"][0])
        UNIT_DQ = n
        for j in range(2):
            units[n] = (rows_pk(a["b_w_dq"][0], 256 * j, 256), 256, cq_ready, TT * (j + 1))
            n += 1
        UNIT_UKV = n
        for j in range(2):
            units[n] = (rows_kp(a["kv_w_ukv"], 1024 * j, 1024), 1024, ukv_ready, 8 * (j + 1))
            n += 1
        UNIT_UQ = n
        for j in range(4):
            units[n] = (rows_kp(a["b_w_uq"][0], 2 * QH * j, 2 * QH), 2 * QH, uq_ready, 3 * (j + 1))
            n += 1
        N_UNITS = tail_units(n, 1, a["b_w_o"][0])

        def unit_cols(n):
            width = units[n][1]
            k = units[n][0].shape[1]
            return ring[:, n % RING, 0:k * width].rearrange("p (k c) -> p k c", c=width)

        def unit_flat(n, size=UNIT):
            return ring[:, n % RING, 0:size]

        def load_units(sp, lo, hi):
            for n in range(lo, hi):
                view, width, _, _ = units[n]
                if n >= RING:
                    _, _, used, value = units[n - RING]
                    sp.wait_ge(used.sem, value)
                if isinstance(view, tuple):
                    parts = [(ring[:, n % RING, j * HALF:(j + 1) * HALF], view[j]) for j in range(2)]
                elif width:
                    dst, k = unit_cols(n), view.shape[1] // 2
                    parts = [(dst[:, :k, :], view[:, :k, :]), (dst[:, k:, :], view[:, k:, :])]
                else:
                    dst, k = unit_flat(n, view.shape[1]), view.shape[1] // 2
                    parts = [(dst[:, :k], view[:, :k]), (dst[:, k:], view[:, k:])]
                for dst, src in parts:
                    sp.dma_start(dst, src).then_inc(slot_loaded[n % RING].sem, 16)

        nxt = [0]

        def unit_wait(eng, n):
            eng.wait_ge(slot_loaded[n % RING].sem, LOADED * (n // RING + 1))

        tr_ready = sem("tr_ready")
        tr_copied = sem("tr_copied")

        def pe_transpose_tokens(pe, block_of, before):
            for n in range(2 * TT):
                tt, half = divmod(n, 2)
                before(tt, half)
                if n >= 2:
                    pe.wait_ge(tr_copied.sem, tr_copied.base + n - 1)
                for j in range(4):
                    last = nc.tensor.transpose(bank[n % 2][:, j * P:(j + 1) * P], block_of(tt, 4 * half + j), ident)
                last.then_inc(tr_ready.sem, 1)

        def act_copy_transposed(act, tt):
            for half in range(2):
                n = 2 * tt + half
                act.wait_ge(tr_ready.sem, tr_ready.base + n + 1)
                nc.scalar.copy(hT[:, half * 4:half * 4 + 4, tt * P:(tt + 1) * P], heads(bank[n % 2][:, :])).then_inc(tr_copied.sem, 1)

        def resid_block(tt, k):
            return resid[:, tt, :].rearrange("p (q k) -> p k q", k=KD)[:, k, :]

        ln_done = sem("ln_done")
        var_ready = sem("var_ready")
        std_ready = sem("std_ready")

        def dve_layer_norm(v, tt, stats, gain, bias):
            s = stats[:, tt, :]
            for half in range(2):
                last = nc.vector.bn_stats(s[:, 6 * half:6 * half + 6], resid[:, tt, half * 512:(half + 1) * 512])
            link(v, "dve", last)
            nc.vector.bn_aggr(s[:, 12:14], s[:, 0:12]).then_inc(var_ready.sem, 1)
            v.wait_ge(std_ready.sem, std_ready.base + tt + 1)
            link(v, "dve", nc.vector.reciprocal(s[:, 14:15], s[:, 14:15]))
            r = resid[:, tt, :]
            link(v, "dve", nc.vector.scalar_tensor_tensor(out=r, in0=r, scalar=s[:, 12:13], in1=gain[:, :], op0=ALU.subtract, op1=ALU.mult))
            nc.vector.scalar_tensor_tensor(out=r, in0=r, scalar=s[:, 14:15], in1=bias[:, :], op0=ALU.mult, op1=ALU.add).then_inc(ln_done.sem, 1)

        def act_layer_norm(act, tt, stats):
            act.wait_ge(var_ready.sem, var_ready.base + tt + 1)
            nc.scalar.activation(stats[:, tt, 14:15], stats[:, tt, 13:14], ACT.Sqrt, bias=eps_col[:, 1:2]).then_inc(std_ready.sem, 1)

        gdn = ExitStack()
        qkT = sb("qkT", [P, 2 * H, T], scope=gdn)
        v_tok = sb("v_tok", [P, TT, H, P], scope=gdn)
        z_gate = sb("z_gate", [P, TT, D], scope=gdn)
        g_tok = sb("g_tok", [P, TT, H], scope=gdn)
        beta = sb("beta", [P, TT, H], scope=gdn)

        proj = ExitStack()
        w_ab = sb("w_ab", [P, KD, 2 * H], scope=proj)
        conv_rows = sb("conv_rows", [CONV * N_QKV, P], scope=proj)
        conv_w = sb("conv_w", [P, CONV, N_QKV], scope=proj)
        a_log = sb("a_log", [P, H], scope=proj)
        dt_bias = sb("dt_bias", [P, H], scope=proj)
        conv_out = sb("conv_out", [P, 2, T], scope=proj)
        conv_act = sb("conv_act", [P, 2, T], scope=proj)
        squares, norm = conv_out, conv_act
        hT_h = sb("hT_h", [P, KD, T], F32R, scope=proj)
        hT_l = sb("hT_l", [P, KD, T], F32R, scope=proj)
        qkv_h = sb("qkv_h", [P, 2, KD // 2, P], F32R, scope=proj)
        qkv_l = sb("qkv_l", [P, 2, KD // 2, P], F32R, scope=proj)
        gate_in = sb("gate_in", [P, TT, H], scope=proj)
        gate_abs = sb("gate_abs", [P, TT, H], scope=proj)

        x_in = [sem(f"x_in{i}") for i in range(TT)]
        const_in = sem("const_in")
        convw_ready = sem("convw_ready")
        ab_ready = sem("ab_ready")
        ab_act = sem("ab_act")
        ab_dve = sem("ab_dve")
        conv_done = sem("conv_done")
        hT_hi = sem("hT_hi")
        first_half_used = sem("first_half_used")
        silu_done = sem("silu_done")
        squared = sem("squared")
        side_ready = sem("side_ready")
        normed = sem("normed")
        norm_done = sem("norm_done")
        eps_set = sem("eps_set")
        v_copied = sem("v_copied")
        z_done = sem("z_done")
        SMALL_0 = 16 * 4

        qkv_bank = (bank[4], bank[5], bank[0])

        def qkv_cols(c, part):
            u, half = divmod(c, 2)
            return unit_cols(u)[:, 4 * part:4 * part + 4, half * P:(half + 1) * P]

        def act_qkv_hi(act, c, parts):
            for part in parts:
                if c % 2 == 0 and part == 0:
                    unit_wait(act, c // 2)
                if c >= 1 and part == 0:
                    act.wait_ge(first_half_used.sem, first_half_used.base + c)
                elif c >= 1:
                    act.wait_ge(qkv_ready.sem, qkv_ready.base + c)
                nc.scalar.copy(qkv_h[:, part, :, :], qkv_cols(c, part)).then_inc(qkv_w_hi.sem, 1)

        def dve_qkv_lo(v, c, parts):
            for part in parts:
                v.wait_ge(qkv_w_hi.sem, qkv_w_hi.base + 2 * c + part + 1)
                nc.vector.tensor_tensor(qkv_l[:, part, :, :], qkv_cols(c, part), qkv_h[:, part, :, :].bitcast(F32), ALU.subtract).then_inc(qkv_w_lo.sem, 1)

        with nc.Block(name="gdn_projections") as block:
            @block.sync
            def _(sp):
                sp.dma_start(const[:, :, :], a["const"].rearrange("p (n q) -> p n q", q=P)).then_inc(const_in.sem, 16)
                for tt in range(TT):
                    sp.dma_start(resid[:, tt, :], a["x"][0, tt * P:(tt + 1) * P, :]).then_inc(x_in[tt].sem, 16)
                load_units(sp, 0, 16 + RING)
                nxt[0] = 16 + RING

            @block.scalar
            def _(act):
                act.dma_start(w_ab[:, :, :], rows_pk(a["a_w_in"][0], 4096, 2 * H)).then_inc(small_in.sem, 16)
                act.dma_start(conv_rows[:, :], a["a_conv_w"][0].rearrange("j (c p) -> (j c) p", p=P)).then_inc(small_in.sem, 16)
                act.dma_start(a_log[:, :], a["a_A_log"][0].partition_broadcast(P)).then_inc(small_in.sem, 16)
                act.dma_start(dt_bias[:, :], a["a_dt_bias"][0].partition_broadcast(P)).then_inc(small_in.sem, 16)
                for n in range(2 * TT):
                    tt, half = divmod(n, 2)
                    act.wait_ge(tr_ready.sem, tr_ready.base + n + 1)
                    k, tok = slice(4 * half, 4 * half + 4), slice(tt * P, (tt + 1) * P)
                    nc.scalar.copy(hT[:, k, tok], heads(bank[n % 2][:, :]))
                    nc.scalar.copy(hT_h[:, k, tok], heads(bank[n % 2][:, :])).then_inc(hT_hi.sem, 1)
                act_qkv_hi(act, 0, range(2))
                act.wait_ge(small_in.sem, small_in.base + SMALL_0)
                nc.scalar.activation(a_log[:, :], a_log[:, :], ACT.Exp).then_inc(ab_act.sem, 1)
                act.wait_ge(ab_ready.sem, ab_ready.base + 1)
                nc.scalar.activation(beta[:, :, :], bank[2][:, 0:TT * 16].rearrange("p (t c) -> p t c", c=16)[:, :, H:16],
                                         ACT.Exp, scale=-1.0).then_inc(ab_act.sem, 1)
                act.wait_ge(ab_dve.sem, ab_dve.base + 1)
                link(act, "act", nc.scalar.activation(gate_abs[:, :, :], gate_in[:, :, :], ACT.Abs))
                link(act, "act", nc.scalar.activation(gate_abs[:, :, :], gate_abs[:, :, :], ACT.Exp, scale=-1.0))
                nc.scalar.activation(gate_abs[:, :, :], gate_abs[:, :, :], ACT.Ln, bias=1.0).then_inc(ab_act.sem, 1)

                def copy_v(h):
                    act.wait_ge(side_ready.sem, side_ready.base + h + 1)
                    nc.scalar.copy(v_tok[:, :, h, :], heads(bank[6 + h % 2][:, :])).then_inc(v_copied.sem, 1)

                act.wait_ge(eps_set.sem, eps_set.base + 2)
                act_qkv_hi(act, 1, [0])
                for c in range(N_QKV):
                    if c + 1 < N_QKV:
                        act_qkv_hi(act, c + 1, [1])
                    if c + 2 < N_QKV:
                        act_qkv_hi(act, c + 2, [0])
                    act.wait_ge(conv_done.sem, conv_done.base + c + 1)
                    if c >= 2 * H + 2:
                        act.wait_ge(side_ready.sem, side_ready.base + c - 2 * H - 1)
                    dst = qkT[:, c, :] if c < 2 * H else conv_act[:, c % 2, :]
                    nc.scalar.activation(dst, conv_out[:, c % 2, :], ACT.Silu).then_inc(silu_done.sem, 1)
                    if c >= 2 * H + 2:
                        copy_v(c - 2 - 2 * H)
                copy_v(H - 2)
                copy_v(H - 1)
                for c in range(2 * H + 1):
                    if c < 2 * H:
                        if c >= 2:
                            act.wait_ge(side_ready.sem, side_ready.base + H + c - 1)
                        nc.scalar.activation(squares[:, c % 2, :], qkT[:, c, :], ACT.Square).then_inc(squared.sem, 1)
                    if c >= 1:
                        act.wait_ge(side_ready.sem, side_ready.base + H + c)
                        if c >= 3:
                            act.wait_ge(normed.sem, normed.base + c - 2)
                        nc.scalar.activation(norm[:, (c - 1) % 2, :], bank[6 + (c - 1) % 2][:, :], ACT.Sqrt, bias=eps_col[:, 0:1]).then_inc(norm_done.sem, 1)

            @block.tensor
            def _(pe):
                pe.wait_ge(const_in.sem, const_in.base + 16)
                pe_transpose_tokens(pe, resid_block, lambda tt, half: pe.wait_ge(x_in[tt].sem, x_in[tt].base + 16))
                pe.wait_ge(small_in.sem, small_in.base + SMALL_0)
                nc.tensor.transpose(bank[3][:, 0:CONV * N_QKV], conv_rows[:, :], const[0:CONV * N_QKV, C_ID, 0:CONV * N_QKV]).then_inc(convw_ready.sem, 1)
                pe.wait_ge(tr_copied.sem, tr_copied.base + 2 * TT)
                for tt in range(TT):
                    for k in range(KD):
                        last = nc.tensor.matmul(bank[2][:, tt * 16:(tt + 1) * 16], lhsT=hT[:, k, tt * P:(tt + 1) * P], rhs=w_ab[:, k, :],
                                                start=k == 0, stop=k == KD - 1)
                last.then_inc(ab_ready.sem, 1)

                def transpose_v(h):
                    c = 2 * H + h
                    pe.wait_ge(silu_done.sem, silu_done.base + c + 1)
                    if h >= 2:
                        pe.wait_ge(v_copied.sem, v_copied.base + h - 1)
                    for tt in range(TT):
                        last = nc.tensor.transpose(bank[6 + h % 2][:, tt * P:(tt + 1) * P], conv_act[:, c % 2, tt * P:(tt + 1) * P], ident)
                    last.then_inc(side_ready.sem, 1)

                def sum_squares(c):
                    pe.wait_ge(squared.sem, squared.base + c + 1)
                    if c >= 2:
                        pe.wait_ge(norm_done.sem, norm_done.base + c - 1)
                    else:
                        pe.wait_ge(v_copied.sem, v_copied.base + H - 1 + c)
                    nc.tensor.matmul(bank[6 + c % 2][:, :], lhsT=plane(C_ONES), rhs=squares[:, c % 2, :], start=True, stop=True).then_inc(side_ready.sem, 1)

                for c in range(N_QKV):
                    if c >= 3:
                        pe.wait_ge(conv_done.sem, conv_done.base + c - 2)
                    out = qkv_bank[c % 3][:, :]
                    for part in range(2):
                        pe.wait_ge(qkv_w_lo.sem, qkv_w_lo.base + 2 * c + part + 1)
                        for j in range(4):
                            k = 4 * part + j
                            nc.tensor.matmul(out, lhsT=qkv_l[:, part, j, :], rhs=hT_h[:, k, :], start=k == 0, stop=False)
                            nc.tensor.matmul(out, lhsT=qkv_h[:, part, j, :], rhs=hT_l[:, k, :], start=False, stop=False)
                            last = nc.tensor.matmul(out, lhsT=qkv_h[:, part, j, :], rhs=hT_h[:, k, :], start=False, stop=k == KD - 1)
                        last.then_inc(qkv_ready.sem if part else first_half_used.sem, 1)
                    if c > 2 * H:
                        transpose_v(c - 1 - 2 * H)
                transpose_v(H - 1)
                for n in range(4 * TT):
                    u, tt = divmod(n, TT)
                    if tt == 0:
                        unit_wait(pe, 12 + u)
                    if n < 2:
                        pe.wait_ge(conv_done.sem, conv_done.base + N_QKV - 1 + n)
                    else:
                        pe.wait_ge(z_done.sem, z_done.base + n - 1)
                    w = unit_cols(12 + u)
                    for k in range(KD):
                        last = nc.tensor.matmul(bank[4 + n % 2][:, 0:256], lhsT=hT[:, k, tt * P:(tt + 1) * P], rhs=w[:, k, :], start=k == 0, stop=k == KD - 1)
                    last.then_inc(z_ready.sem, 1)
                    sum_squares(n)

            @block.vector
            def _(v):
                for n in range(2 * TT):
                    tt, half = divmod(n, 2)
                    v.wait_ge(hT_hi.sem, hT_hi.base + n + 1)
                    k, tok = slice(4 * half, 4 * half + 4), slice(tt * P, (tt + 1) * P)
                    nc.vector.tensor_tensor(hT_l[:, k, tok], heads(bank[n % 2][:, :]), hT_h[:, k, tok].bitcast(F32), ALU.subtract).then_inc(tr_copied.sem, 1)
                dve_qkv_lo(v, 0, range(2))
                v.wait_ge(convw_ready.sem, convw_ready.base + 1)
                link(v, "dve", nc.vector.tensor_copy(conv_w[:, :, :], bank[3][:, 0:CONV * N_QKV].rearrange("p (j c) -> p j c", c=N_QKV)))
                v.wait_ge(ab_ready.sem, ab_ready.base + 1)
                ab = bank[2][:, 0:TT * 16].rearrange("p (t c) -> p t c", c=16)
                v.wait_ge(ab_act.sem, ab_act.base + 2)
                nc.vector.tensor_tensor(gate_in[:, :, :], ab[:, :, 0:H], dt_bias[:, :].unsqueeze(1).to_broadcast([P, TT, H]), ALU.add).then_inc(ab_dve.sem, 1)
                link(v, "dve", nc.vector.tensor_single_scalar(beta[:, :, :], beta[:, :, :], 1.0, ALU.add))
                link(v, "dve", nc.vector.reciprocal(beta[:, :, :], beta[:, :, :]))
                v.wait_ge(ab_act.sem, ab_act.base + 3)
                link(v, "dve", nc.vector.scalar_tensor_tensor(out=gate_in[:, :, :], in0=gate_in[:, :, :], scalar=0.0, in1=gate_abs[:, :, :], op0=ALU.max, op1=ALU.add))
                link(v, "dve", nc.vector.scalar_tensor_tensor(out=g_tok[:, :, :], in0=gate_in[:, :, :], scalar=-1.0, in1=a_log[:, :].unsqueeze(1).to_broadcast([P, TT, H]), op0=ALU.mult, op1=ALU.mult))

                def copy_z(n):
                    u, tt = divmod(n, TT)
                    v.wait_ge(z_ready.sem, z_ready.base + n + 1)
                    nc.vector.tensor_copy(z_gate[:, tt, u * 256:(u + 1) * 256], bank[4 + n % 2][:, 0:256]).then_inc(z_done.sem, 1)

                def normalise(c):
                    v.wait_ge(norm_done.sem, norm_done.base + c + 1)
                    half = norm[:, c % 2, :]
                    link(v, "dve", nc.vector.reciprocal(half, half))
                    nc.vector.scalar_tensor_tensor(out=qkT[:, c, :], in0=qkT[:, c, :], scalar=P ** -0.5 if c < H else 1.0,
                                                       in1=half, op0=ALU.mult, op1=ALU.mult).then_inc(normed.sem, 1)

                dve_qkv_lo(v, 1, [0])
                for c in range(N_QKV):
                    if c + 1 < N_QKV:
                        dve_qkv_lo(v, c + 1, [1])
                    v.wait_ge(qkv_ready.sem, qkv_ready.base + c + 1)
                    if c >= 2:
                        v.wait_ge(silu_done.sem, silu_done.base + c - 1)
                    x, y = qkv_bank[c % 3], conv_out[:, c % 2, :]
                    link(v, "dve", nc.vector.tensor_scalar(y, x[:, :], conv_w[:, CONV - 1, c:c + 1], None, ALU.mult))
                    for back in range(1, CONV):
                        if back == CONV - 1 and c + 2 < N_QKV:
                            dve_qkv_lo(v, c + 2, [0])
                        w = conv_w[:, CONV - 1 - back, c:c + 1]
                        ins = nc.vector.scalar_tensor_tensor(out=y[:, back:T], in0=x[:, 0:T - back], scalar=w, in1=y[:, back:T], op0=ALU.mult, op1=ALU.add)
                        if back < CONV - 1:
                            link(v, "dve", ins)
                    ins.then_inc(conv_done.sem, 1)
                for n in range(4 * TT + 1):
                    if n < 4 * TT:
                        copy_z(n)
                    if n >= 1:
                        normalise(n - 1)

            @block.gpsimd
            def _(pool):
                nc.gpsimd.memset(eps_col[:, 0:1], EPS).then_inc(eps_set.sem, 1)
                nc.gpsimd.memset(eps_col[:, 1:2], LN_EPS).then_inc(eps_set.sem, 1)
        proj.close()

        core = ExitStack()

        def pair(name):
            return [sb(f"{name}{g}", [P, HG, P], scope=core) for g in range(2)]

        def spare(j):
            return [heads(hT[:, j + g, :]) for g in range(2)]

        eg_row, decay_kg, attn_kbg, lower_sdec = spare(0), spare(2), spare(4), spare(6)
        attnT, lowT_vb, mask0_wT, mask1, X_u, Y, prod_vnew, q_decayed, state = (
            pair(n) for n in ("attnT", "lowT_vb", "mask0_wT", "mask1", "X_u", "Y", "prod_vnew", "q_decayed", "state"))
        masked = [mask0_wT, mask1]
        gcol = sb("gcol", [P, 2, HG], scope=core)
        ecol = sb("ecol", [P, 2, 2 * HG], scope=core)
        beta_eg = sb("beta_eg", [P, 2, HG], scope=core)

        core_sems = {n: sem(n) for n in (
            "gates_ready", "gates_exp", "decay_arg", "decay_exp", "kk_ready", "lower_done", "lowT_ready", "lowT_copied",
            "xy_done", "mask_done", "prod_ready", "prod_copied", "xy_ready", "ktok_ready", "k_scaled", "vq_scaled",
            "uw_ready", "uw_copied", "ws_ready", "vnew_done", "scan_ready", "state_decayed", "state_done", "o_copied")}
        (gates_ready, gates_exp, decay_arg, decay_exp, kk_ready, lower_done, lowT_ready, lowT_copied,
         xy_done, mask_done, prod_ready, prod_copied, xy_ready, ktok_ready, k_scaled, vq_scaled,
         uw_ready, uw_copied, ws_ready, vnew_done, scan_ready, state_decayed, state_done, o_copied) = core_sems.values()
        NS = 2 * TT
        LV = LEVELS - 1

        def ev(s, c):
            tt, g = divmod(s, 2)
            return 4 * tt + 2 * c + g

        def lev(s, level, per):
            tt, g = divmod(s, 2)
            return 2 * per * tt + 2 * level + g

        def banks(g):
            return [bank[4 * g + i] for i in range(4)]

        with nc.Block(name="gdn_delta_rule") as block:
            @block.tensor
            def _(pe):
                for tt in range(TT):
                    pairs = [(2 * tt + g, g, banks(g)) for g in range(2)]
                    tok = slice(tt * P, (tt + 1) * P)
                    for s, g, b in pairs:
                        if tt > 0:
                            pe.wait_ge(vnew_done.sem, vnew_done.base + ev(s - 2, 1) + 1)
                            pe.wait_ge(o_copied.sem, o_copied.base + ev(s - 2, 1) + 1)
                        for h in range(HG):
                            nc.tensor.matmul(b[0][:, h * P:(h + 1) * P], lhsT=g_tok[:, tt, HG * g + h:HG * g + h + 1].to_broadcast([P, P]), rhs=plane(C_CUM), start=True, stop=True)
                        gs = g_tok[:, tt, HG * g:HG * g + HG]
                        nc.tensor.matmul(b[3][:, 0:HG], lhsT=plane(C_CUM), rhs=gs, start=True, stop=True)
                        nc.tensor.matmul(b[3][:, HG:2 * HG], lhsT=plane(C_AFTER), rhs=gs, start=True, stop=True).then_inc(gates_ready.sem, 1)
                    for s, g, b in pairs:
                        if tt > 0:
                            pe.wait_ge(state_done.sem, state_done.base + ev(s - 2, 1) + 1)
                            pe.wait_ge(uw_copied.sem, uw_copied.base + s - 1)
                        for h in range(HG):
                            q, k = qkT[:, HG * g + h, tok], qkT[:, H + HG * g + h, tok]
                            nc.tensor.matmul(b[1][:, h * P:(h + 1) * P], lhsT=k, rhs=k, start=True, stop=True)
                            last = nc.tensor.matmul(b[2][:, h * P:(h + 1) * P], lhsT=q, rhs=k, start=True, stop=True)
                        last.then_inc(kk_ready.sem, 1)
                    for s, g, b in pairs:
                        pe.wait_ge(lower_done.sem, lower_done.base + s + 1)
                        pe.wait_ge(gates_exp.sem, gates_exp.base + s + 1)
                        for h in range(HG):
                            nc.tensor.transpose(b[0][:, h * P:(h + 1) * P], attn_kbg[g][:, h, :], ident)
                            last = nc.tensor.transpose(b[3][:, h * P:(h + 1) * P], lower_sdec[g][:, h, :], ident)
                        last.then_inc(lowT_ready.sem, 1)
                    for s, g, b in pairs:
                        pe.wait_ge(lowT_copied.sem, lowT_copied.base + s + 1)
                        for h in range(HG):
                            last = nc.tensor.transpose(b[0][:, h * P:(h + 1) * P], qkT[:, H + HG * g + h, tok], ident)
                        last.then_inc(ktok_ready.sem, 1)
                    for level in range(LV):
                        for s, g, b in pairs:
                            pe.wait_ge(xy_done.sem, xy_done.base + lev(s, level, LEVELS) + 1)
                            pe.wait_ge(mask_done.sem, mask_done.base + lev(s, level, LV) + 1)
                            for h in range(HG):
                                last = nc.tensor.matmul(b[1][:, h * P:(h + 1) * P], lhsT=masked[level % 2][g][:, h, :], rhs=X_u[g][:, h, :], start=True, stop=True)
                            last.then_inc(prod_ready.sem, 1)
                        for s, g, b in pairs:
                            pe.wait_ge(prod_copied.sem, prod_copied.base + lev(s, level, LV) + 1)
                            for h in range(HG):
                                last = nc.tensor.matmul(b[2][:, h * P:(h + 1) * P], lhsT=prod_vnew[g][:, h, :], rhs=Y[g][:, h, :], start=True, stop=True)
                                if level < LV - 1:
                                    last = nc.tensor.matmul(b[3][:, h * P:(h + 1) * P], lhsT=Y[g][:, h, :], rhs=prod_vnew[g][:, h, :], start=True, stop=True)
                            last.then_inc(xy_ready.sem, 1)
                    for s, g, b in pairs:
                        pe.wait_ge(xy_done.sem, xy_done.base + lev(s, LV, LEVELS) + 1)
                        pe.wait_ge(k_scaled.sem, k_scaled.base + s + 1)
                        pe.wait_ge(vq_scaled.sem, vq_scaled.base + s + 1)
                        for h in range(HG):
                            nc.tensor.matmul(b[1][:, h * P:(h + 1) * P], lhsT=Y[g][:, h, :], rhs=lowT_vb[g][:, h, :], start=True, stop=True)
                            last = nc.tensor.matmul(b[2][:, h * P:(h + 1) * P], lhsT=attn_kbg[g][:, h, :], rhs=Y[g][:, h, :], start=True, stop=True)
                        last.then_inc(uw_ready.sem, 1)
                    for c in range(2):
                        R = slice(c * CHUNK, (c + 1) * CHUNK)
                        for s, g, b in pairs:
                            pe.wait_ge(uw_copied.sem, uw_copied.base + s + 1)
                            if ev(s, c) >= 2:
                                pe.wait_ge(state_done.sem, state_done.base + ev(s, c) - 1)
                            else:
                                pe.wait_ge(state_decayed.sem, state_decayed.base + 2)
                            if c == 1:
                                pe.wait_ge(vnew_done.sem, vnew_done.base + ev(s, 0) + 1)
                            for h in range(HG):
                                last = nc.tensor.matmul(b[0][R, h * P:(h + 1) * P], lhsT=mask0_wT[g][:, h, R], rhs=state[g][:, h, :], start=True, stop=True)
                            last.then_inc(ws_ready.sem, 1)
                        for s, g, b in pairs:
                            pe.wait_ge(vnew_done.sem, vnew_done.base + ev(s, c) + 1)
                            for h in range(HG):
                                o = b[3][R, h * P:(h + 1) * P]
                                nc.tensor.matmul(o, lhsT=q_decayed[g][:, h, R], rhs=state[g][:, h, :], start=True, stop=False)
                                nc.tensor.matmul(o, lhsT=attnT[g][R, h, R], rhs=prod_vnew[g][R, h, :], start=False, stop=True)
                            for h in range(HG):
                                last = nc.tensor.matmul(b[1][:, h * P:(h + 1) * P], lhsT=decay_kg[g][R, h, :], rhs=prod_vnew[g][R, h, :], start=True, stop=True)
                            last.then_inc(scan_ready.sem, 1)

            @block.scalar
            def _(act):
                for tt in range(TT):
                    pairs = [(2 * tt + g, g, banks(g)) for g in range(2)]
                    for s, g, b in pairs:
                        act.wait_ge(gates_ready.sem, gates_ready.base + s + 1)
                        act.wait_ge(decay_arg.sem, decay_arg.base + s + 1)
                        nc.scalar.activation(eg_row[g], heads(b[0][:, :]), ACT.Exp)
                        nc.scalar.activation(ecol[:, g, :], b[3][:, 0:2 * HG], ACT.Exp)
                        nc.scalar.activation(decay_kg[g], decay_kg[g], ACT.Exp, scale=-1.0).then_inc(gates_exp.sem, 1)
                    for s, g, b in pairs:
                        act.wait_ge(lowT_ready.sem, lowT_ready.base + s + 1)
                        nc.scalar.copy(attnT[g][:, :, :], heads(b[0][:, :]))
                        nc.scalar.copy(lowT_vb[g][:, :, :], heads(b[3][:, :])).then_inc(lowT_copied.sem, 1)
                    for level in range(LV):
                        for s, g, b in pairs:
                            act.wait_ge(prod_ready.sem, prod_ready.base + lev(s, level, LV) + 1)
                            nc.scalar.copy(prod_vnew[g][:, :, :], heads(b[1][:, :])).then_inc(prod_copied.sem, 1)
                    for s, g, b in pairs:
                        act.wait_ge(uw_ready.sem, uw_ready.base + s + 1)
                        nc.scalar.copy(X_u[g][:, :, :], heads(b[1][:, :]))
                        nc.scalar.copy(mask0_wT[g][:, :, :], heads(b[2][:, :])).then_inc(uw_copied.sem, 1)
                    for c in range(2):
                        R = slice(c * CHUNK, (c + 1) * CHUNK)
                        for s, g, b in pairs:
                            act.wait_ge(scan_ready.sem, scan_ready.base + ev(s, c) + 1)
                            nc.scalar.copy(v_tok[R, tt, HG * g:HG * g + HG, :], heads(b[3][R, :])).then_inc(o_copied.sem, 1)

            @block.vector
            def _(v):
                for tt in range(TT):
                    pairs = [(2 * tt + g, g, banks(g)) for g in range(2)]
                    for s, g, b in pairs:
                        v.wait_ge(gates_ready.sem, gates_ready.base + s + 1)
                        link(v, "dve", nc.vector.tensor_copy(gcol[:, g, :], b[3][:, 0:HG]))
                        for h in range(HG):
                            last = nc.vector.tensor_scalar(decay_kg[g][:, h, :], b[0][:, h * P:(h + 1) * P], gcol[:, g, h:h + 1], 0.0, ALU.subtract, ALU.max)
                        last.then_inc(decay_arg.sem, 1)
                    for s, g, b in pairs:
                        v.wait_ge(kk_ready.sem, kk_ready.base + s + 1)
                        v.wait_ge(gates_exp.sem, gates_exp.base + s + 1)
                        link(v, "dve", nc.vector.tensor_tensor(decay_kg[g], decay_kg[g], planes(C_INCL), ALU.mult))
                        nc.vector.tensor_tensor(attn_kbg[g], heads(b[2][:, :]), decay_kg[g], ALU.mult)
                        link(v, "dve", nc.vector.tensor_tensor(lower_sdec[g], heads(b[1][:, :]), decay_kg[g], ALU.mult))
                        nc.vector.tensor_tensor(lower_sdec[g], lower_sdec[g], beta[:, tt, HG * g:HG * g + HG].unsqueeze(2).to_broadcast([P, HG, P]), ALU.mult).then_inc(lower_done.sem, 1)
                    for s, g, b in pairs:
                        v.wait_ge(lowT_copied.sem, lowT_copied.base + s + 1)
                        v.wait_ge(lower_done.sem, lower_done.base + s + 1)
                        nc.vector.tensor_tensor(X_u[g][:, :, :], lower_sdec[g], planes(C_M0), ALU.mult)
                        link(v, "dve", nc.vector.tensor_tensor(Y[g][:, :, :], lowT_vb[g][:, :, :], planes(C_MT), ALU.mult))
                        nc.vector.tensor_tensor(X_u[g][:, :, :], planes(C_ID), X_u[g][:, :, :], ALU.subtract)
                        nc.vector.tensor_tensor(Y[g][:, :, :], planes(C_ID), Y[g][:, :, :], ALU.subtract).then_inc(xy_done.sem, 1)
                    for level in range(LV):
                        for s, g, b in pairs:
                            if level == 0:
                                v.wait_ge(ktok_ready.sem, ktok_ready.base + s + 1)
                                bc = [P, HG, P]
                                link(v, "dve", nc.vector.tensor_tensor(beta_eg[:, g, :], beta[:, tt, HG * g:HG * g + HG], ecol[:, g, 0:HG], ALU.mult))
                                nc.vector.tensor_tensor(decay_kg[g], heads(b[0][:, :]), ecol[:, g, HG:2 * HG].unsqueeze(2).to_broadcast(bc), ALU.mult)
                                nc.vector.tensor_tensor(attn_kbg[g], heads(b[0][:, :]), beta_eg[:, g, :].unsqueeze(2).to_broadcast(bc), ALU.mult).then_inc(k_scaled.sem, 1)
                            v.wait_ge(xy_ready.sem, xy_ready.base + lev(s, level, LV) + 1)
                            if level < LV - 1:
                                nc.vector.tensor_tensor(X_u[g][:, :, :], X_u[g][:, :, :], heads(b[3][:, :]), ALU.subtract)
                            nc.vector.tensor_tensor(Y[g][:, :, :], Y[g][:, :, :], heads(b[2][:, :]), ALU.subtract).then_inc(xy_done.sem, 1)
                    for c in range(2):
                        R = slice(c * CHUNK, (c + 1) * CHUNK)
                        for s, g, b in pairs:
                            v.wait_ge(ws_ready.sem, ws_ready.base + ev(s, c) + 1)
                            nc.vector.tensor_tensor(prod_vnew[g][R, :, :], X_u[g][R, :, :], heads(b[0][R, :]), ALU.subtract).then_inc(vnew_done.sem, 1)
                        for s, g, b in pairs:
                            v.wait_ge(scan_ready.sem, scan_ready.base + ev(s, c) + 1)
                            v.wait_ge(state_decayed.sem, state_decayed.base + 2 + ev(s, c) + 1)
                            nc.vector.tensor_tensor(state[g][:, :, :], lower_sdec[g], heads(b[1][:, :]), ALU.add).then_inc(state_done.sem, 1)

            @block.gpsimd
            def _(pool):
                for g in range(2):
                    nc.gpsimd.memset(state[g][:, :, :], 0.0).then_inc(state_decayed.sem, 1)
                pool.wait_ge(state_decayed.sem, 2)
                for tt in range(TT):
                    pairs = [(2 * tt + g, g, banks(g)) for g in range(2)]
                    for level in range(LV):
                        for s, g, b in pairs:
                            if level == 0:
                                pool.wait_ge(lowT_copied.sem, lowT_copied.base + s + 1)
                            if level >= 2:
                                pool.wait_ge(prod_ready.sem, prod_ready.base + lev(s, level - 2, LV) + 1)
                            nc.gpsimd.tensor_tensor(masked[level % 2][g][:, :, :], lowT_vb[g][:, :, :], planes(C_MT + 1 + level), ALU.mult).then_inc(mask_done.sem, 1)
                    for s, g, b in pairs:
                        pool.wait_ge(mask_done.sem, mask_done.base + lev(s, LV - 1, LV) + 1)
                        pool.wait_ge(xy_done.sem, xy_done.base + lev(s, 0, LEVELS) + 1)
                        nc.gpsimd.tensor_tensor(lowT_vb[g][:, :, :], v_tok[:, tt, HG * g:HG * g + HG, :], beta[:, tt, HG * g:HG * g + HG].unsqueeze(2).to_broadcast([P, HG, P]), ALU.mult)
                        nc.gpsimd.tensor_tensor(q_decayed[g][:, :, :], qkT[:, HG * g:HG * g + HG, tt * P:(tt + 1) * P], eg_row[g], ALU.mult).then_inc(vq_scaled.sem, 1)
                    for c in range(2):
                        last_tok = (c + 1) * CHUNK - 1
                        for s, g, b in pairs:
                            if ev(s, c) >= 2:
                                pool.wait_ge(state_done.sem, state_done.base + ev(s, c) - 1)
                            nc.gpsimd.tensor_tensor(lower_sdec[g], state[g][:, :, :], eg_row[g][:, :, last_tok:last_tok + 1].to_broadcast([P, HG, P]), ALU.mult).then_inc(state_decayed.sem, 1)
        core.close()

        mixed_added = sem("mixed_added")

        def mixer_out(name, layer, mixT, prepare):
            ln = ExitStack()
            gain = sb(f"ln1_gain_{layer}", [P, D], scope=ln)
            bias = sb(f"ln1_bias_{layer}", [P, D], scope=ln)
            stats = sb(f"ln1_stats_{layer}", [P, TT, 16], scope=ln)
            u0 = UNIT_OUT[layer]
            with nc.Block(name=name) as block:
                @block.sync
                def _(sp):
                    sp.dma_start(gain[:, :], a["ln1_g"][layer].partition_broadcast(P)).then_inc(small_in.sem, 16)
                    sp.dma_start(bias[:, :], a["ln1_b"][layer].partition_broadcast(P)).then_inc(small_in.sem, 16)
                    load_units(sp, nxt[0], u0 + 8)
                    nxt[0] = u0 + 8

                @block.tensor
                def _(pe):
                    prepare["pe"](pe, 0)
                    for n in range(4 * TT):
                        tt, u = divmod(n, 4)
                        if u == 2 and tt + 1 < TT:
                            prepare["pe"](pe, tt + 1)
                        if u == 0:
                            prepare["pe_copied"](pe, tt)
                        if tt == 0:
                            unit_wait(pe, u0 + u)
                        if n >= 2:
                            pe.wait_ge(mixed_added.sem, mixed_added.base + n - 1)
                        w = unit_cols(u0 + u)
                        for k in range(KD):
                            last = nc.tensor.matmul(bank[4 + n % 2][:, 0:256], lhsT=mixT[:, k, tt * P:(tt + 1) * P], rhs=w[:, k, :], start=k == 0, stop=k == KD - 1)
                        last.then_inc(mix_ready.sem, 1)

                @block.vector
                def _(v):
                    prepare["dve"](v, 0)
                    v.wait_ge(small_in.sem, small_in.base + 32)
                    for n in range(4 * TT):
                        tt, u = divmod(n, 4)
                        if u == 0 and tt + 1 < TT:
                            prepare["dve"](v, tt + 1)
                        v.wait_ge(mix_ready.sem, mix_ready.base + n + 1)
                        r = resid[:, tt, u * 256:(u + 1) * 256]
                        nc.vector.scalar_tensor_tensor(out=r, in0=r, scalar=ALPHA, in1=bank[4 + n % 2][:, 0:256], op0=ALU.mult, op1=ALU.add).then_inc(mixed_added.sem, 1)
                        if u == 1 and tt >= 1:
                            v.wait_ge(mixed_added.sem, mixed_added.base + 4 * tt)
                            dve_layer_norm(v, tt - 1, stats, gain, bias)
                    v.wait_ge(mixed_added.sem, mixed_added.base + 4 * TT)
                    dve_layer_norm(v, TT - 1, stats, gain, bias)

                @block.scalar
                def _(act):
                    prepare["act"](act, 0)
                    prepare["act_copy"](act, 0)
                    for tt in range(TT):
                        if tt + 1 < TT:
                            prepare["act"](act, tt + 1)
                        if tt >= 1:
                            act_layer_norm(act, tt - 1, stats)
                        if tt + 1 < TT:
                            prepare["act_copy"](act, tt + 1)
                    act_layer_norm(act, TT - 1, stats)
            small_in.base += 32
            mix_ready.base += 4 * TT
            mixed_added.base += 4 * TT
            for c in (ln_done, var_ready, std_ready):
                c.base += TT
            ln.close()

        small_in.base = SMALL_0
        tr_ready.base += 2 * TT
        tr_copied.base += 2 * TT
        gated = ExitStack()
        o_sq = sb("o_sq", [P, 2, D], scope=gated)
        o_rms = sb("o_rms", [P, TT, H], scope=gated)
        onorm = sb("onorm", [P, P], scope=gated)
        gated_ready = sem("gated_ready")
        onorm_in = sem("onorm_in")
        rms_in = sem("rms_in")
        rms_out = sem("rms_out")

        z_silu = sem("z_silu")

        def dve_gated(v, tt):
            o, sq = v_tok[:, tt, :, :], heads(o_sq[:, tt % 2, :])
            if tt == 0:
                v.wait_ge(onorm_in.sem, onorm_in.base + 16)
            link(v, "dve", nc.vector.tensor_tensor(sq, o, o, ALU.mult))
            link(v, "dve", nc.vector.tensor_reduce(o_rms[:, tt, :], sq, AX.X, ALU.add))
            nc.vector.tensor_scalar(o_rms[:, tt, :], o_rms[:, tt, :], 1.0 / P, EPS, ALU.mult, ALU.add).then_inc(rms_in.sem, 1)
            v.wait_ge(rms_out.sem, rms_out.base + tt + 1)
            link(v, "dve", nc.vector.reciprocal(o_rms[:, tt, :], o_rms[:, tt, :]))
            link(v, "dve", nc.vector.tensor_tensor(sq, o, o_rms[:, tt, :].unsqueeze(2).to_broadcast([P, H, P]), ALU.mult))
            link(v, "dve", nc.vector.tensor_tensor(sq, sq, onorm[:, :].unsqueeze(1).to_broadcast([P, H, P]), ALU.mult))
            v.wait_ge(z_silu.sem, z_silu.base + tt + 1)
            nc.vector.tensor_tensor(o, sq, heads(z_gate[:, tt, :]), ALU.mult).then_inc(gated_ready.sem, 1)

        def pe_gated(pe, tt):
            pe.wait_ge(gated_ready.sem, gated_ready.base + tt + 1)
            for half in range(2):
                n = 2 * tt + half
                if n >= 2:
                    pe.wait_ge(tr_copied.sem, tr_copied.base + n - 1)
                for j in range(4):
                    last = nc.tensor.transpose(bank[n % 2][:, j * P:(j + 1) * P], v_tok[:, tt, 4 * half + j, :], ident)
                last.then_inc(tr_ready.sem, 1)

        def act_gated(act, tt):
            if tt == 0:
                act.dma_start(onorm[:, :], a["a_onorm_w"][0].partition_broadcast(P)).then_inc(onorm_in.sem, 16)
                nc.scalar.activation(z_gate[:, 0, :], z_gate[:, 0, :], ACT.Silu).then_inc(z_silu.sem, 1)
            act.wait_ge(rms_in.sem, rms_in.base + tt + 1)
            nc.scalar.activation(o_rms[:, tt, :], o_rms[:, tt, :], ACT.Sqrt).then_inc(rms_out.sem, 1)
            if tt == 0:
                for t in range(1, TT):
                    nc.scalar.activation(z_gate[:, t, :], z_gate[:, t, :], ACT.Silu).then_inc(z_silu.sem, 1)

        def act_gated_copy(act, tt):
            for half in range(2):
                n = 2 * tt + half
                act.wait_ge(tr_ready.sem, tr_ready.base + n + 1)
                nc.scalar.copy(hT[:, half * 4:half * 4 + 4, tt * P:(tt + 1) * P], heads(bank[n % 2][:, :])).then_inc(tr_copied.sem, 1)

        prepare = {"pe": pe_gated, "dve": dve_gated, "act": act_gated, "act_copy": act_gated_copy, "pe_copied": lambda pe, tt: pe.wait_ge(tr_copied.sem, tr_copied.base + 2 * tt + 2)}
        mixer_out("gdn_out", 0, hT, prepare)
        tr_ready.base += 2 * TT
        tr_copied.base += 2 * TT
        gated.close()
        gdn.close()

        names = ("perm_done", "scores_done", "sel_done", "rank_ready", "rank_done", "xg_cleared", "silu2_done", "hm_done",
                 "hmT_ready", "hmT_copied", "sum_done", "rows_stored0", "rows_stored1", "onehot_done", "list_ready", "list_copied",
                 "xgT_ready", "xgT_hi", "hmT_hi", "xgT_copied", "out_list_done", "y_done", "scattered", "pool_tick", "bias_in",
                 "gathered0", "gathered1", "sum_stored0", "sum_stored1")
        m_ = {name: sem(name) for name in names}
        (perm_done, scores_done, sel_done, rank_ready, rank_done, xg_cleared, silu2_done, hm_done,
         hmT_ready, hmT_copied, sum_done, rows_stored0, rows_stored1, onehot_done, list_ready, list_copied,
         xgT_ready, xgT_hi, hmT_hi, xgT_copied, out_list_done, y_done, scattered, pool_tick, bias_in,
         gathered0, gathered1, sum_stored0, sum_stored1) = m_.values()
        gathered, sum_stored, rows_stored = (gathered0, gathered1), (sum_stored0, sum_stored1), (rows_stored0, rows_stored1)
        LOOP = (E - 8) // 4

        def moe(layer):
            ln = ln2[layer]
            gain = sb(f"ln2_gain_{layer}", [P, D], scope=ln)
            bias = sb(f"ln2_bias_{layer}", [P, D], scope=ln)
            stats = sb(f"ln2_stats_{layer}", [P, TT, 16], scope=ln)
            mo = ExitStack()
            router_bias = sb(f"router_bias_{layer}", [P, E], scope=mo)
            scores = sb(f"scores_{layer}", [P, TT, E], scope=mo)
            biased = sb(f"biased_{layer}", [P, TT, E], scope=mo)
            picked = sb(f"picked_{layer}", [P, TT, E], scope=mo)
            pairs_hi = sb(f"pairs_hi_{layer}", [P, TT * GROUPS, PER // 2], scope=mo)
            pairs_lo = sb(f"pairs_lo_{layer}", [P, TT * GROUPS, PER // 2], scope=mo)
            four_hi = sb(f"four_hi_{layer}", [P, TT * GROUPS, 2], scope=mo)
            four_lo = sb(f"four_lo_{layer}", [P, TT * GROUPS, 2], scope=mo)
            four_tmp = sb(f"four_tmp_{layer}", [P, TT * GROUPS, 2], scope=mo)
            group_score = sb(f"group_score_{layer}", [P, TT, GROUPS], scope=mo)
            group_tmp = sb(f"group_tmp_{layer}", [P, TT, GROUPS], scope=mo)
            ahead = sb(f"ahead_{layer}", [P, TT, GROUPS, GROUPS], scope=mo)
            ties = sb(f"ties_{layer}", [P, TT, GROUPS, GROUPS], scope=mo)
            top8 = sb(f"top8_{layer}", [P, TT, 8], scope=mo)
            w_sum = sb(f"w_sum_{layer}", [P, TT], scope=mo)
            entry = sb(f"entry_{layer}", [P, TT, E, 2], scope=mo)
            rank = sb(f"rank_{layer}", [P, TT, E], scope=mo)
            most = sb(f"most_{layer}", [P, 1], scope=mo)
            most_int = sb(f"most_int_{layer}", [P, 1], I32, scope=mo)
            counts = sb(f"counts_{layer}", [P, E], I32, scope=mo)
            onehot = sb(f"onehot_{layer}", [P, 2, TT, P], scope=mo)
            list_idx = sb(f"list_idx_{layer}", [P, 4], U32, scope=mo)
            list_w = sb(f"list_w_{layer}", [P, 4], scope=mo)
            out_idx = sb(f"out_idx_{layer}", [P, 2], U32, scope=mo)
            out_w = sb(f"out_w_{layer}", [P, 2], scope=mo)
            xg = [sb(f"xg{b}_{layer}", [P, D], scope=mo) for b in range(2)]
            xgT_h = sb(f"xgT_h_{layer}", [P, 2, KD, P], F32R, scope=mo)
            xgT_l = sb(f"xgT_l_{layer}", [P, 2, KD, P], F32R, scope=mo)
            gu_h = sb(f"gu_h_{layer}", [P, CH_GU, 2, CH // 2], F32R, scope=mo)
            gu_l = sb(f"gu_l_{layer}", [P, CH_GU, 2, CH // 2], F32R, scope=mo)
            down_h = sb(f"down_h_{layer}", [P, CH_DOWN, CH], F32R, scope=mo)
            down_l = sb(f"down_l_{layer}", [P, CH_DOWN, CH], F32R, scope=mo)
            silu_g = sb(f"silu_g_{layer}", [P, 2, FE], scope=mo)
            hm = sb(f"hm_{layer}", [P, 2, FE], scope=mo)
            hmT_h = sb(f"hmT_h_{layer}", [P, 2, 2, P], F32R, scope=mo)
            hmT_l = sb(f"hmT_l_{layer}", [P, 2, 2, P], F32R, scope=mo)
            y = [sb(f"y{b}_{layer}", [P, D], scope=mo) for b in range(2)]
            U = UNIT_EXPERT[layer]
            US = UNIT_SHARED[layer]

            def item_units(r, i, shared):
                n0 = US if shared else U + 3 * r

                def arrived(eng, j):
                    n = n0 + j
                    eng.wait_ge(slot_loaded[n % RING].sem, LOADED * (n // RING + 1) + 2 * LOADED * i)
                return n0 % RING, (n0 + 2) % RING, arrived

            def gate_up_cols(slot, c0, width):
                j, c0 = divmod(c0, HALF)
                return ring[:, slot + j, :].rearrange("p (g c) -> p g c", g=2)[:, :, c0:c0 + width]

            def bump(pool):
                pool.sem_inc(pool_tick.sem, 1)

            def pe_gather_list(pe, r, i):
                pe.wait_ge(onehot_done.sem, onehot_done.base + r + 1 + 4 * i)
                if r >= 1:
                    pe.wait_ge(list_copied.sem, list_copied.base + r + 4 * i)
                for tt in range(TT):
                    last = nc.tensor.matmul(bank[5][:, 0:2], lhsT=onehot[:, r % 2, tt, :], rhs=entry[:, tt, bass.ds(r + 4 * i, 1), :].rearrange("p e c -> p (e c)"),
                                            start=tt == 0, stop=tt == TT - 1)
                last.then_inc(list_ready.sem, 1)

            def pe_rows_T(pe, r, i):
                g = gathered[r % 2]
                pe.wait_ge(g.sem, g.base + 16 * (r // 2 + 1) + 32 * i)
                for half in range(2):
                    if r >= 1:
                        pe.wait_ge(xgT_copied.sem, xgT_copied.base + 2 * r - 1 + half + 8 * i)
                    for j in range(4):
                        k = 4 * half + j
                        last = nc.tensor.transpose(bank[2 + half][:, j * P:(j + 1) * P], xg[r % 2][:, k * P:(k + 1) * P], ident)
                    last.then_inc(xgT_ready.sem, 1)

            def pe_gate_up(pe, r, i, shared=False):
                m = r if shared else TT + r
                gate_slot, _, arrived = item_units(r, i, shared)
                if shared:
                    if r == 0:
                        arrived(pe, 0)
                        arrived(pe, 1)
                else:
                    pe.wait_ge(xgT_copied.sem, xgT_copied.base + 2 * r + 2 + 8 * i)
                if m >= 2:
                    pe.wait_ge(hm_done.sem, hm_done.base + m - 1 + 4 * i)
                out = bank[m % 2][:, :]
                for k in range(KD):
                    c, part = divmod(k, KD // CH_GU)
                    if shared:
                        last = nc.tensor.matmul(out, lhsT=hT[:, k, r * P:(r + 1) * P], rhs=gate_up_cols(gate_slot, k * FE, FE), start=k == 0, stop=k == KD - 1)
                    else:
                        if part == 0:
                            pe.wait_ge(gu_lo.sem, gu_lo.base + CH_GU * r + c + 1 + 4 * CH_GU * i)
                        xh, xl = xgT_h[:, r % 2, k, :], xgT_l[:, r % 2, k, :]
                        wh, wl = gu_h[:, c, :, part * FE:(part + 1) * FE], gu_l[:, c, :, part * FE:(part + 1) * FE]
                        nc.tensor.matmul(out, lhsT=xl, rhs=wh, start=k == 0, stop=False)
                        nc.tensor.matmul(out, lhsT=xh, rhs=wl, start=False, stop=False)
                        last = nc.tensor.matmul(out, lhsT=xh, rhs=wh, start=False, stop=k == KD - 1)
                    if part == KD // CH_GU - 1:
                        last.then_inc(gu_ready.sem, 1)

            def pe_hm_T(pe, r, i, shared=False):
                m = r if shared else TT + r
                pe.wait_ge(hm_done.sem, hm_done.base + m + 1 + 4 * i)
                if m >= 1:
                    pe.wait_ge(hmT_copied.sem, hmT_copied.base + m + 4 * i)
                for j in range(2):
                    last = nc.tensor.transpose(bank[4][:, j * P:(j + 1) * P], hm[:, m % 2, j * P:(j + 1) * P], ident)
                last.then_inc(hmT_ready.sem, 1)

            def pe_down(pe, r, i, shared=False):
                m = r if shared else TT + r
                s = 0 if shared else r + 1
                pe.wait_ge(down_lo.sem, down_lo.base + CH_DOWN * (s + 1) + 4 * CH_DOWN * i)
                pe.wait_ge(hmT_copied.sem, hmT_copied.base + m + 1 + 4 * i)
                if 1 <= m <= TT:
                    pe.wait_ge(sum_done.sem, sum_done.base + m)
                elif m > TT:
                    pe.wait_ge(y_done.sem, y_done.base + r + 4 * i)
                for half in range(2):
                    for j in range(2):
                        out = bank[6 + half][:, :]
                        xh, xl = hmT_h[:, m % 2, j, :], hmT_l[:, m % 2, j, :]
                        wh, wl = down_h[:, j, half * 512:half * 512 + 512], down_l[:, j, half * 512:half * 512 + 512]
                        nc.tensor.matmul(out, lhsT=xl, rhs=wh, start=j == 0, stop=False)
                        nc.tensor.matmul(out, lhsT=xh, rhs=wl, start=False, stop=False)
                        last = nc.tensor.matmul(out, lhsT=xh, rhs=wh, start=False, stop=j == 1)
                last.then_inc(down_ready.sem, 1)

            def pe_step(pe, r, i, last=False):
                if not last or r + 1 < E:
                    pe_rows_T(pe, r + 1, i)
                pe_gate_up(pe, r, i)
                if not last or r + 3 < E:
                    pe_gather_list(pe, r + 3, i)
                if r >= 1:
                    pe_down(pe, r - 1, i)
                else:
                    pe_down(pe, TT - 1, 0, True)
                pe_hm_T(pe, r, i)

            def act_rows_T(act, r, i):
                for half in range(2):
                    act.wait_ge(xgT_ready.sem, xgT_ready.base + 2 * r + 1 + half + 8 * i)
                    if half == 0 and r >= 2:
                        act.wait_ge(gu_ready.sem, gu_ready.base + CH_GU * (TT + r - 1) + 4 * CH_GU * i)
                    nc.scalar.copy(xgT_h[:, r % 2, 4 * half:4 * half + 4, :], heads(bank[2 + half][:, :])).then_inc(xgT_hi.sem, 1)

            def act_gu_hi(act, r, i, parts):
                gate_slot, _, arrived = item_units(r, i, False)
                for c in parts:
                    if c % 2 == 0:
                        arrived(act, c // 2)
                    if r >= 1:
                        act.wait_ge(gu_ready.sem, gu_ready.base + CH_GU * (TT + r - 1) + c + 1 + 4 * CH_GU * i)
                    nc.scalar.copy(gu_h[:, c, :, :], gate_up_cols(gate_slot, c * CH // 2, CH // 2)).then_inc(gu_hi.sem, 1)

            def act_down_hi(act, r, i, shared=False):
                _, down_slot, arrived = item_units(r, i, shared)
                arrived(act, 2)
                if not shared:
                    act.wait_ge(down_ready.sem, down_ready.base + TT + r + 4 * i)
                for c in range(CH_DOWN):
                    nc.scalar.copy(down_h[:, c, :], ring[:, down_slot, c * CH:(c + 1) * CH]).then_inc(down_hi.sem, 1)

            def act_silu(act, r, i, shared=False):
                m = r if shared else TT + r
                act.wait_ge(gu_ready.sem, gu_ready.base + CH_GU * (m + 1) + 4 * CH_GU * i)
                if m >= 2:
                    act.wait_ge(hm_done.sem, hm_done.base + m - 1 + 4 * i)
                nc.scalar.activation(silu_g[:, m % 2, :], bank[m % 2][:, 0:FE], ACT.Silu).then_inc(silu2_done.sem, 1)

            def act_hm_T(act, r, i, shared=False):
                m = r if shared else TT + r
                act.wait_ge(hmT_ready.sem, hmT_ready.base + m + 1 + 4 * i)
                if m >= 2:
                    act.wait_ge(down_ready.sem, down_ready.base + m - 1 + 4 * i)
                nc.scalar.copy(hmT_h[:, m % 2, :, :], heads(bank[4][:, 0:2 * P])).then_inc(hmT_hi.sem, 1)

            def act_result(act, r, i):
                act.wait_ge(out_list_done.sem, out_list_done.base + r + 1 + 4 * i)
                act.wait_ge(down_ready.sem, down_ready.base + TT + r + 1 + 4 * i)
                if r < 2:
                    act.wait_ge(sum_stored[r % 2].sem, sum_stored[r % 2].base + 32)
                nc.scalar.activation(y[r % 2][:, 0:512], bank[6][:, :], ACT.Copy, scale=out_w[:, r % 2:r % 2 + 1])
                nc.scalar.activation(y[r % 2][:, 512:1024], bank[7][:, :], ACT.Copy, scale=out_w[:, r % 2:r % 2 + 1]).then_inc(y_done.sem, 1)

            def act_store_sum(act, tt):
                act.wait_ge(sum_done.sem, sum_done.base + tt + 1)
                act.dma_start(moe_sum[tt * P:(tt + 1) * P, :], y[tt % 2][:, :]).then_inc(sum_stored[tt % 2].sem, 16)

            def act_step(act, r, i, last=False):
                if not last or r + 1 < E:
                    act_rows_T(act, r + 1, i)
                if r >= 1:
                    act_hm_T(act, r - 1, i)
                if not last or r + 1 < E:
                    act_gu_hi(act, r + 1, i, range(CH_GU - 1))
                act_silu(act, r, i)
                if not last or r + 1 < E:
                    act_gu_hi(act, r + 1, i, [CH_GU - 1])
                act_down_hi(act, r, i)
                if r >= 1:
                    act_result(act, r - 1, i)
                else:
                    act_store_sum(act, TT - 1)

            def dve_onehot(v, r, i):
                if r >= 2:
                    v.wait_ge(list_ready.sem, list_ready.base + r - 1 + 4 * i)
                nc.vector.tensor_tensor(onehot[:, r % 2, :, :], planes(C_IOTA, TT), rank[:, :, bass.ds(r + 4 * i, 1)].to_broadcast([P, TT, P]), ALU.is_equal).then_inc(onehot_done.sem, 1)

            def dve_list(v, r, i):
                v.wait_ge(list_ready.sem, list_ready.base + r + 1 + 4 * i)
                if r >= 4:
                    v.wait_ge(gathered[r % 2].sem, gathered[r % 2].base + 16 * (r // 2 - 1) + 32 * i)
                    v.wait_ge(out_list_done.sem, out_list_done.base + r - 3 + 4 * i)
                nc.vector.tensor_single_scalar(list_idx[:, r % 4:r % 4 + 1], bank[5][:, 0:1], float(T), ALU.add)
                nc.vector.tensor_copy(list_w[:, r % 4:r % 4 + 1], bank[5][:, 1:2]).then_inc(list_copied.sem, 1)

            def dve_out_list(v, r, i):
                v.wait_ge(list_copied.sem, list_copied.base + r + 1 + 4 * i)
                if r >= 2:
                    v.wait_ge(y_done.sem, y_done.base + r - 1 + 4 * i)
                    v.wait_ge(scattered.sem, scattered.base + 16 * (r - 1) + 64 * i)
                nc.vector.tensor_copy(out_idx[:, r % 2:r % 2 + 1], list_idx[:, r % 4:r % 4 + 1])
                nc.vector.tensor_copy(out_w[:, r % 2:r % 2 + 1], list_w[:, r % 4:r % 4 + 1]).then_inc(out_list_done.sem, 1)

            def dve_product(v, r, i, shared=False):
                m = r if shared else TT + r
                v.wait_ge(silu2_done.sem, silu2_done.base + m + 1 + 4 * i)
                if m >= 2:
                    v.wait_ge(hmT_ready.sem, hmT_ready.base + m - 1 + 4 * i)
                nc.vector.tensor_tensor(hm[:, m % 2, :].rearrange("p (j q) -> p q j", j=2), silu_g[:, m % 2, :].rearrange("p (q j) -> p q j", j=2),
                                            bank[m % 2][:, FE:2 * FE].rearrange("p (q j) -> p q j", j=2), ALU.mult).then_inc(hm_done.sem, 1)

            def dve_rows_T(v, r, i):
                for half in range(2):
                    v.wait_ge(xgT_hi.sem, xgT_hi.base + 2 * r + 1 + half + 8 * i)
                    k = slice(4 * half, 4 * half + 4)
                    nc.vector.tensor_tensor(xgT_l[:, r % 2, k, :], heads(bank[2 + half][:, :]), xgT_h[:, r % 2, k, :].bitcast(F32), ALU.subtract).then_inc(xgT_copied.sem, 1)

            def dve_hm_T(v, r, i, shared=False):
                m = r if shared else TT + r
                v.wait_ge(hmT_hi.sem, hmT_hi.base + m + 1 + 4 * i)
                nc.vector.tensor_tensor(hmT_l[:, m % 2, :, :], heads(bank[4][:, 0:2 * P]), hmT_h[:, m % 2, :, :].bitcast(F32), ALU.subtract).then_inc(hmT_copied.sem, 1)

            def dve_gu_lo(v, r, i, parts):
                gate_slot, _, _ = item_units(r, i, False)
                for c in parts:
                    v.wait_ge(gu_hi.sem, gu_hi.base + CH_GU * r + c + 1 + 4 * CH_GU * i)
                    nc.vector.tensor_tensor(gu_l[:, c, :, :], gate_up_cols(gate_slot, c * CH // 2, CH // 2), gu_h[:, c, :, :].bitcast(F32), ALU.subtract).then_inc(gu_lo.sem, 1)

            def dve_down_lo(v, r, i, shared=False):
                _, down_slot, _ = item_units(r, i, shared)
                s = 0 if shared else r + 1
                v.wait_ge(down_hi.sem, down_hi.base + CH_DOWN * s + 1 + 4 * CH_DOWN * i)
                nc.vector.tensor_tensor(down_l[:, 0, :], ring[:, down_slot, 0:CH], down_h[:, 0, :].bitcast(F32), ALU.subtract).then_inc(down_lo.sem, 1)

            def dve_sum(v, tt):
                v.wait_ge(down_ready.sem, down_ready.base + tt + 1)
                if tt == 0:
                    for c in rows_stored:
                        v.wait_ge(c.sem, c.base + 32)
                if tt >= 2:
                    v.wait_ge(sum_stored[tt % 2].sem, sum_stored[tt % 2].base + 16)
                for half in range(2):
                    c = slice(half * 512, half * 512 + 512)
                    ins = nc.vector.scalar_tensor_tensor(out=y[tt % 2][:, c], in0=resid[:, tt, c], scalar=ALPHA, in1=bank[6 + half][:, :], op0=ALU.mult, op1=ALU.add)
                ins.then_inc(sum_done.sem, 1)

            def dve_step(v, r, i, last=False):
                if not last or r + 3 < E:
                    dve_onehot(v, r + 3, i)
                if r >= 1:
                    dve_down_lo(v, r - 1, i)
                if not last or r + 1 < E:
                    dve_rows_T(v, r + 1, i)
                if r >= 1:
                    dve_hm_T(v, r - 1, i)
                if not last or r + 1 < E:
                    dve_gu_lo(v, r + 1, i, range(CH_GU - 1))
                dve_product(v, r, i)
                if not last or r + 1 < E:
                    dve_gu_lo(v, r + 1, i, [CH_GU - 1])
                if r >= 1:
                    dve_out_list(v, r - 1, i)
                if not last or r + 3 < E:
                    dve_list(v, r + 3, i)
                if r == 0:
                    dve_sum(v, TT - 1)

            def dve_route(v):
                L = lambda ins: link(v, "dve", ins)
                tt_ = nc.vector.tensor_tensor
                v.wait_ge(bias_in.sem, bias_in.base + 16)
                v.wait_ge(scores_done.sem, scores_done.base + 1)
                L(tt_(biased[:, :, :], scores[:, :, :], router_bias[:, :].unsqueeze(1).to_broadcast([P, TT, E]), ALU.add))
                b8 = biased[:, :, :].rearrange("p t (g e) -> p (t g) e", g=GROUPS)
                tt_(pairs_hi[:, :, :], b8[:, :, 0:4], b8[:, :, 4:8], ALU.max)
                L(tt_(pairs_lo[:, :, :], b8[:, :, 0:4], b8[:, :, 4:8], ALU.min))
                tt_(four_hi[:, :, :], pairs_hi[:, :, 0:2], pairs_hi[:, :, 2:4], ALU.max)
                tt_(four_lo[:, :, :], pairs_hi[:, :, 0:2], pairs_hi[:, :, 2:4], ALU.min)
                L(tt_(four_tmp[:, :, :], pairs_lo[:, :, 0:2], pairs_lo[:, :, 2:4], ALU.max))
                L(tt_(four_lo[:, :, :], four_lo[:, :, :], four_tmp[:, :, :], ALU.max))
                gs = group_score[:, :, :].rearrange("p t g -> p (t g)").unsqueeze(2)
                gt = group_tmp[:, :, :].rearrange("p t g -> p (t g)").unsqueeze(2)
                tt_(gs, four_hi[:, :, 0:1], four_hi[:, :, 1:2], ALU.max)
                tt_(gt, four_hi[:, :, 0:1], four_hi[:, :, 1:2], ALU.min)
                L(tt_(four_tmp[:, :, 0:1], four_lo[:, :, 0:1], four_lo[:, :, 1:2], ALU.max))
                L(tt_(gt, gt, four_tmp[:, :, 0:1], ALU.max))
                L(tt_(gs, gs, gt, ALU.add))
                other = group_score[:, :, :].unsqueeze(2).to_broadcast([P, TT, GROUPS, GROUPS])
                own = group_score[:, :, :].unsqueeze(3).to_broadcast([P, TT, GROUPS, GROUPS])
                low = const[:, C_LOW, 0:GROUPS * GROUPS].unsqueeze(1).to_broadcast([P, TT, GROUPS * GROUPS])
                tt_(ahead[:, :, :, :], other, own, ALU.is_gt)
                L(tt_(ties[:, :, :, :], other, own, ALU.is_equal))
                flat_ties = ties[:, :, :, :].rearrange("p t g h -> p t (g h)")
                L(tt_(flat_ties, flat_ties, low, ALU.mult))
                L(tt_(ahead[:, :, :, :], ahead[:, :, :, :], ties[:, :, :, :], ALU.add))
                L(nc.vector.tensor_reduce(group_tmp[:, :, :], ahead[:, :, :, :], AX.X, ALU.add))
                L(nc.vector.tensor_single_scalar(group_tmp[:, :, :], group_tmp[:, :, :], float(TOP_GROUPS), ALU.is_lt))
                keep = group_tmp[:, :, :].rearrange("p t g -> p (t g)").unsqueeze(2).to_broadcast([P, TT * GROUPS, PER])
                L(nc.vector.tensor_scalar(group_score[:, :, :], group_tmp[:, :, :], 1.0, -NEG, ALU.subtract, ALU.mult))
                L(tt_(b8, b8, keep, ALU.mult))
                L(tt_(b8, b8, group_score[:, :, :].rearrange("p t g -> p (t g)").unsqueeze(2).to_broadcast([P, TT * GROUPS, PER]), ALU.add))
                for tt in range(TT):
                    last = nc.vector.max(top8[:, tt, :], biased[:, tt, :])
                L(last)
                for tt in range(TT):
                    last = nc.vector.match_replace(out=picked[:, tt, :], in_to_replace=top8[:, tt, :], in_values=biased[:, tt, :], imm_value=1.1 * NEG)
                L(last)
                tt_(picked[:, :, :], picked[:, :, :], biased[:, :, :], ALU.not_equal).then_inc(sel_done.sem, 1)
                v.wait_ge(sel_done.sem, sel_done.base + 1)
                L(tt_(biased[:, :, :], scores[:, :, :], picked[:, :, :], ALU.mult))
                L(nc.vector.tensor_reduce(w_sum[:, :], biased[:, :, :], AX.X, ALU.add))
                L(nc.vector.tensor_single_scalar(w_sum[:, :], w_sum[:, :], 1e-20, ALU.add))
                L(nc.vector.reciprocal(w_sum[:, :], w_sum[:, :]))
                L(nc.vector.tensor_single_scalar(w_sum[:, :], w_sum[:, :], ROUTED_SCALE, ALU.mult))
                tt_(entry[:, :, :, 1], biased[:, :, :], w_sum[:, :].unsqueeze(2).to_broadcast([P, TT, E]), ALU.mult)
                L(nc.vector.tensor_copy(entry[:, :, :, 0], const[:, C_TOK, 0:TT].unsqueeze(2).to_broadcast([P, TT, E])))

            def dve_rank(v):
                L = lambda ins: link(v, "dve", ins)
                v.wait_ge(rank_ready.sem, rank_ready.base + 1)
                L(nc.vector.scalar_tensor_tensor(out=rank[:, :, :], in0=bank[3][:, 0:TT * E].rearrange("p (t e) -> p t e", e=E), scalar=1.0, in1=picked[:, :, :], op0=ALU.add, op1=ALU.mult))
                L(nc.vector.tensor_single_scalar(rank[:, :, :], rank[:, :, :], -1.0, ALU.add))
                nc.vector.tensor_copy(counts[:, :], bank[3][:, TT * E:TT * E + E])
                L(nc.vector.reduce_max(most[:, :], bank[3][:, TT * E:TT * E + E], AX.X))
                nc.vector.tensor_copy(most_int[:, :], most[:, :]).then_inc(rank_done.sem, 1)

            def pool_rows(pool, r, i, move, sizes=ROWS_MOVED, tokens=None):
                if tokens is None:
                    tokens = pool.value_load(counts[0:1, bass.ds(r + 4 * i, 1)])
                if len(sizes) == 1:
                    move(sizes[0])
                    return
                with pool.If(tokens > sizes[-2]):
                    move(sizes[-1])
                with pool.Else():
                    pool_rows(pool, r, i, move, sizes[:-1], tokens)

            def pool_down_lo(pool, r, i, shared=False):
                _, down_slot, _ = item_units(r, i, shared)
                s = 0 if shared else r + 1
                pool.wait_ge(down_hi.sem, down_hi.base + CH_DOWN * (s + 1) + 4 * CH_DOWN * i)
                nc.gpsimd.tensor_tensor(down_l[:, 1, :], ring[:, down_slot, CH:2 * CH], down_h[:, 1, :].bitcast(F32), ALU.subtract).then_inc(down_lo.sem, 1)

            def pool_gather(pool, r, i):
                pool.wait_ge(list_copied.sem, list_copied.base + r + 1 + 4 * i)
                bump(pool)
                if r >= 2:
                    pool.wait_ge(xgT_ready.sem, xgT_ready.base + 2 * r - 2 + 8 * i)
                    bump(pool)

                def move(n):
                    pool.indirect_dma_start(out=xg[r % 2][0:n, :], out_offset=None, in_=h_rows, in_offset=bass.IndirectOffsetOnAxis(ap=list_idx[0:n, r % 4:r % 4 + 1], axis=0),
                                                   bounds_check=T - 1, oob_is_err=False).then_inc(gathered[r % 2].sem, 16)
                pool_rows(pool, r, i, move)

            def pool_scatter(pool, r, i):
                pool.wait_ge(y_done.sem, y_done.base + r + 1 + 4 * i)
                bump(pool)
                if r >= 1:
                    pool.wait_ge(scattered.sem, scattered.base + 16 * r + 64 * i)
                    bump(pool)

                def move(n):
                    pool.indirect_dma_start(out=moe_sum, out_offset=bass.IndirectOffsetOnAxis(ap=out_idx[0:n, r % 2:r % 2 + 1], axis=0), in_=y[r % 2][0:n, :], in_offset=None,
                                                   bounds_check=T - 1, oob_is_err=False, compute_op=ALU.add).then_inc(scattered.sem, 16)
                pool_rows(pool, r, i, move)

            def pool_step(pool, r, i, last=False):
                if not last or r + 3 < E:
                    pool_gather(pool, r + 3, i)
                pool_down_lo(pool, r, i)
                if r >= 1:
                    pool_scatter(pool, r - 1, i)

            def steps(eng, step):
                for r in range(5):
                    step(eng, r, 0)
                with eng.Fori(0, LOOP) as i:
                    for r in range(5, 9):
                        step(eng, r, i)
                for r in range(E - 3, E):
                    step(eng, r, 0, True)

            with nc.Block(name=f"moe{layer}") as block:
                @block.sync
                def _(sp):
                    sp.dma_start(router_bias[:, :], a["moe_router_bias"][layer].partition_broadcast(P)).then_inc(bias_in.sem, 16)
                    for tt in range(TT):
                        sp.wait_ge(perm_done.sem, perm_done.base + tt + 1)
                        sp.dma_start(h_rows[tt * P:(tt + 1) * P, :], y[tt % 2][:, :]).then_inc(rows_stored[tt % 2].sem, 16)
                    sp.dma_start(gain[:, :], a["ln2_g"][layer].partition_broadcast(P)).then_inc(small_in.sem, 16)
                    sp.dma_start(bias[:, :], a["ln2_b"][layer].partition_broadcast(P)).then_inc(small_in.sem, 16)
                    load_units(sp, nxt[0], U)
                    nxt[0] = U + 3 * E
                    weights = [a[w][layer].rearrange("e (p k) c -> e p (k c)", p=P) for w in ("moe_w_gate", "moe_w_up", "moe_w_down")]

                    def load_expert(r, i):
                        for j in range(3):
                            n = U + 3 * r + j
                            _, _, used, value = units[n - RING]
                            sp.wait_ge(used.sem, value + 4 * (CH_GU if used is gu_lo else CH_DOWN) * i)
                            for h in range(2):
                                w, c0 = (weights[h], j * HALF) if j < 2 else (weights[2], h * HALF)
                                sp.dma_start(ring[:, n % RING, h * HALF:(h + 1) * HALF], w[bass.ds(r + 4 * i, 1), :, c0:c0 + HALF].rearrange("e p c -> (e p) c")).then_inc(slot_loaded[n % RING].sem, 16)

                    load_expert(0, 0)
                    load_expert(1, 0)
                    with sp.Fori(0, (E - 4) // 4) as i:
                        for r in range(2, 6):
                            load_expert(r, i)
                    load_expert(E - 2, 0)
                    load_expert(E - 1, 0)

                @block.tensor
                def _(pe):
                    pe_transpose_tokens(pe, lambda tt, k: y[tt % 2][:, k * P:(k + 1) * P], lambda tt, half: pe.wait_ge(perm_done.sem, perm_done.base + tt + 1))
                    pe.wait_ge(tr_copied.sem, tr_copied.base + 2 * TT)
                    unit_wait(pe, UNIT_ROUTER[layer])
                    w = unit_flat(UNIT_ROUTER[layer], KD * E).rearrange("p (k e) -> p k e", e=E)
                    for tt in range(TT):
                        for k in range(KD):
                            last = nc.tensor.matmul(bank[2][:, tt * E:(tt + 1) * E], lhsT=hT[:, k, tt * P:(tt + 1) * P], rhs=w[:, k, :], start=k == 0, stop=k == KD - 1)
                    last.then_inc(router_ready.sem, 1)
                    pe_gate_up(pe, 0, 0, True)
                    for tt in range(TT):
                        if tt == 2:
                            pe.wait_ge(sel_done.sem, sel_done.base + 1)
                            for t in range(TT):
                                for s in range(t + 1):
                                    nc.tensor.matmul(bank[3][:, t * E:(t + 1) * E], lhsT=plane(C_BEFORE if s == t else C_ONES), rhs=picked[:, s, :], start=s == 0, stop=s == t)
                            for s in range(TT):
                                last = nc.tensor.matmul(bank[3][:, TT * E:TT * E + E], lhsT=plane(C_ONES), rhs=picked[:, s, :], start=s == 0, stop=s == TT - 1)
                            last.then_inc(rank_ready.sem, 1)
                        if tt + 1 < TT:
                            pe_gate_up(pe, tt + 1, 0, True)
                        if tt == 2:
                            pe_gather_list(pe, 0, 0)
                            pe_gather_list(pe, 1, 0)
                        pe_hm_T(pe, tt, 0, True)
                        if tt >= 1:
                            pe_down(pe, tt - 1, 0, True)
                        if tt == 2:
                            pe_gather_list(pe, 2, 0)
                    pe.wait_ge(rank_done.sem, rank_done.base + 1)
                    pe_rows_T(pe, 0, 0)
                    steps(pe, pe_step)
                    pe_down(pe, E - 1, 0)

                @block.scalar
                def _(act):
                    for tt in range(TT):
                        if tt >= 2:
                            act.wait_ge(rows_stored[tt % 2].sem, rows_stored[tt % 2].base + 16)
                            act.wait_ge(tr_ready.sem, tr_ready.base + 2 * (tt - 1))
                        nc.scalar.copy(y[tt % 2][:, :].rearrange("p (k q) -> p k q", k=KD), resid[:, tt, :].rearrange("p (q k) -> p k q", k=KD)).then_inc(perm_done.sem, 1)
                        if tt >= 1:
                            act_copy_transposed(act, tt - 1)
                    act_copy_transposed(act, TT - 1)
                    act_down_hi(act, 0, 0, True)
                    act.wait_ge(router_ready.sem, router_ready.base + 1)
                    nc.scalar.activation(scores[:, :, :], bank[2][:, 0:TT * E].rearrange("p (t e) -> p t e", e=E), ACT.Sigmoid).then_inc(scores_done.sem, 1)
                    for tt in range(TT):
                        act_silu(act, tt, 0, True)
                        act_hm_T(act, tt, 0, True)
                        if tt >= 1:
                            act_store_sum(act, tt - 1)
                        if tt == 2:
                            act_gu_hi(act, 0, 0, range(CH_GU))
                    act_rows_T(act, 0, 0)
                    steps(act, act_step)
                    act_hm_T(act, E - 1, 0)
                    act_result(act, E - 1, 0)

                @block.vector
                def _(v):
                    for b in range(2):
                        nc.vector.memset(xg[b][:, :], 0.0).then_inc(xg_cleared.sem, 1)
                    dve_down_lo(v, 0, 0, True)
                    dve_route(v)
                    for tt in range(TT):
                        if tt == 2:
                            dve_rank(v)
                            dve_onehot(v, 0, 0)
                            dve_onehot(v, 1, 0)
                        dve_product(v, tt, 0, True)
                        if tt == 2:
                            dve_list(v, 0, 0)
                            dve_onehot(v, 2, 0)
                            dve_list(v, 1, 0)
                        dve_hm_T(v, tt, 0, True)
                        if tt >= 1:
                            dve_sum(v, tt - 1)
                        if tt == 2:
                            dve_list(v, 2, 0)
                            dve_gu_lo(v, 0, 0, range(CH_GU))
                    dve_rows_T(v, 0, 0)
                    steps(v, dve_step)
                    dve_down_lo(v, E - 1, 0)
                    dve_hm_T(v, E - 1, 0)
                    dve_out_list(v, E - 1, 0)

                @block.gpsimd
                def _(pool):
                    pool_down_lo(pool, 0, 0, True)
                    pool.wait_ge(xg_cleared.sem, xg_cleared.base + 2)
                    bump(pool)
                    for c in rows_stored:
                        pool.wait_ge(c.sem, c.base + 32)
                        bump(pool)
                    pool.wait_ge(rank_done.sem, rank_done.base + 1)
                    for r in range(3):
                        pool_gather(pool, r, 0)
                    for c in sum_stored:
                        pool.wait_ge(c.sem, c.base + 32)
                        bump(pool)
                    steps(pool, pool_step)
                    pool_scatter(pool, E - 1, 0)
                    pool.wait_ge(scattered.sem, scattered.base + 16 * E)
            for c, n in ((perm_done, TT), (scores_done, 1), (sel_done, 1), (rank_ready, 1), (rank_done, 1), (xg_cleared, 2), (silu2_done, TT + E),
                         (hm_done, TT + E), (hmT_ready, TT + E), (hmT_copied, TT + E), (sum_done, TT), (rows_stored0, 32), (rows_stored1, 32), (onehot_done, E),
                         (list_ready, E), (list_copied, E), (xgT_ready, 2 * E), (xgT_copied, 2 * E), (out_list_done, E), (y_done, E),
                         (scattered, 16 * E), (bias_in, 16), (gathered0, 8 * E), (gathered1, 8 * E), (sum_stored0, 32), (sum_stored1, 32),
                         (gu_ready, CH_GU * (TT + E)), (down_ready, TT + E), (gu_hi, CH_GU * E), (gu_lo, CH_GU * E), (down_hi, CH_DOWN * (1 + E)), (down_lo, CH_DOWN * (1 + E)),
                         (xgT_hi, 2 * E), (hmT_hi, TT + E), (router_ready, 1), (tr_ready, 2 * TT), (tr_copied, 2 * TT)):
                c.base += n

            if layer == 0:
                ov = {name: sem(f"over_{name}") for name in (
                    "onehot", "list", "index", "gathered", "rowsT", "rowsT_copied", "gate_up", "silu", "product", "hmT", "hmT_copied", "down", "result", "added")}
            else:
                ov = {"onehot": onehot_done, "list": list_ready, "index": list_copied, "gathered": gathered0, "rowsT": xgT_ready, "rowsT_copied": xgT_copied,
                      "gate_up": gu_ready, "silu": silu2_done, "product": hm_done, "hmT": hmT_ready, "hmT_copied": hmT_copied, "down": down_ready,
                      "result": y_done, "added": scattered}
            ov["free"], ov["weights"] = sem(f"over_free{layer}"), sem(f"over_weights{layer}")

            def over_passes(eng, before_pass, expert):
                most_tokens = eng.value_load(most_int[0:1, 0:1])
                for p in range(1, T // CAP):
                    with eng.If(most_tokens > CAP * p):
                        before_pass()
                        with eng.Fori(0, E) as e:
                            expert(E * (p - 1), e)

            with nc.Block(name=f"moe_overflow{layer}") as block:
                @block.sync
                def _(sp):
                    weights = [a[w][layer].rearrange("e (p k) c -> e p (k c)", p=P) for w in ("moe_w_gate", "moe_w_up", "moe_w_down")]

                    def expert(n, e):
                        sp.wait_ge(ov["free"].sem, ov["free"].base + n + 1 + e)
                        for j in range(3):
                            sp.dma_start(ring[:, j, :], weights[j][bass.ds(e, 1), :, :].rearrange("e p c -> (e p) c")).then_inc(ov["weights"].sem, 16)
                    over_passes(sp, lambda: None, expert)

                @block.vector
                def _(v):
                    own = [0]

                    def next_ranks():
                        nc.vector.tensor_single_scalar(rank[:, :, :], rank[:, :, :], -float(CAP), ALU.add).then_inc(ov["product"].sem, 1)
                        own[0] += 1
                        v.wait_ge(ov["product"].sem, ov["product"].base + E * (own[0] - 1) + own[0])

                    def expert(n, e):
                        v.wait_ge(ov["free"].sem, ov["free"].base + n + 1 + e)
                        nc.vector.tensor_tensor(onehot[:, 0, :, :], planes(C_IOTA, TT), rank[:, :, bass.ds(e, 1)].to_broadcast([P, TT, P]), ALU.is_equal).then_inc(ov["onehot"].sem, 1)
                        v.wait_ge(ov["list"].sem, ov["list"].base + n + 1 + e)
                        nc.vector.tensor_single_scalar(list_idx[:, 0:1], bank[5][:, 0:1], float(T), ALU.add)
                        nc.vector.tensor_copy(list_w[:, 0:1], bank[5][:, 1:2]).then_inc(ov["index"].sem, 1)
                        v.wait_ge(ov["silu"].sem, ov["silu"].base + n + 1 + e)
                        nc.vector.tensor_tensor(hm[:, 0, :].rearrange("p (j q) -> p q j", j=2), silu_g[:, 0, :].rearrange("p (q j) -> p q j", j=2),
                                                    bank[0][:, FE:2 * FE].rearrange("p (q j) -> p q j", j=2), ALU.mult).then_inc(ov["product"].sem, 1)
                    over_passes(v, next_ranks, expert)

                @block.tensor
                def _(pe):
                    def expert(n, e):
                        passes = n // E + 1
                        pe.wait_ge(ov["onehot"].sem, ov["onehot"].base + n + 1 + e)
                        for tt in range(TT):
                            last = nc.tensor.matmul(bank[5][:, 0:2], lhsT=onehot[:, 0, tt, :], rhs=entry[:, tt, bass.ds(e, 1), :].rearrange("p e c -> p (e c)"), start=tt == 0, stop=tt == TT - 1)
                        last.then_inc(ov["list"].sem, 1)
                        pe.wait_ge(ov["gathered"].sem, ov["gathered"].base + 16 * (n + 1) + 16 * e)
                        for k in range(KD):
                            last = nc.tensor.transpose(bank[2 + k // 4][:, k % 4 * P:(k % 4 + 1) * P], xg[0][:, k * P:(k + 1) * P], ident)
                        last.then_inc(ov["rowsT"].sem, 1)
                        pe.wait_ge(ov["rowsT_copied"].sem, ov["rowsT_copied"].base + n + 1 + e)
                        pe.wait_ge(ov["weights"].sem, ov["weights"].base + 48 * (n + 1) + 48 * e)
                        for k in range(KD):
                            last = nc.tensor.matmul(bank[0][:, :], lhsT=hT[:, k, 0:P], rhs=ring[:, 0:2, k * FE:(k + 1) * FE], start=k == 0, stop=k == KD - 1)
                        last.then_inc(ov["gate_up"].sem, 1)
                        pe.wait_ge(ov["product"].sem, ov["product"].base + n + 1 + passes + e)
                        for j in range(2):
                            last = nc.tensor.transpose(bank[4][:, j * P:(j + 1) * P], hm[:, 0, j * P:(j + 1) * P], ident)
                        last.then_inc(ov["hmT"].sem, 1)
                        pe.wait_ge(ov["hmT_copied"].sem, ov["hmT_copied"].base + n + 1 + e)
                        for half in range(2):
                            for j in range(2):
                                c = j * D + half * 512
                                last = nc.tensor.matmul(bank[6 + half][:, :], lhsT=hT[:, j, P:2 * P], rhs=ring[:, 2, c:c + 512], start=j == 0, stop=j == 1)
                        last.then_inc(ov["down"].sem, 1)
                    over_passes(pe, lambda: None, expert)

                @block.scalar
                def _(act):
                    def expert(n, e):
                        act.wait_ge(ov["rowsT"].sem, ov["rowsT"].base + n + 1 + e)
                        nc.scalar.copy(hT[:, 0:4, 0:P], heads(bank[2][:, :]))
                        nc.scalar.copy(hT[:, 4:8, 0:P], heads(bank[3][:, :])).then_inc(ov["rowsT_copied"].sem, 1)
                        act.wait_ge(ov["gate_up"].sem, ov["gate_up"].base + n + 1 + e)
                        nc.scalar.activation(silu_g[:, 0, :], bank[0][:, 0:FE], ACT.Silu).then_inc(ov["silu"].sem, 1)
                        act.wait_ge(ov["hmT"].sem, ov["hmT"].base + n + 1 + e)
                        nc.scalar.copy(hT[:, 0:2, P:2 * P], heads(bank[4][:, 0:2 * P])).then_inc(ov["hmT_copied"].sem, 1)
                        act.wait_ge(ov["down"].sem, ov["down"].base + n + 1 + e)
                        nc.scalar.activation(y[0][:, 0:512], bank[6][:, :], ACT.Copy, scale=list_w[:, 0:1])
                        nc.scalar.activation(y[0][:, 512:1024], bank[7][:, :], ACT.Copy, scale=list_w[:, 0:1]).then_inc(ov["result"].sem, 1)
                    over_passes(act, lambda: None, expert)

                @block.gpsimd
                def _(pool):
                    pool.sem_inc(ov["free"].sem, 1)

                    def expert(n, e):
                        pool.wait_ge(ov["index"].sem, ov["index"].base + n + 1 + e)
                        bump(pool)
                        pool.indirect_dma_start(out=xg[0][:, :], out_offset=None, in_=h_rows, in_offset=bass.IndirectOffsetOnAxis(ap=list_idx[:, 0:1], axis=0),
                                                       bounds_check=T - 1, oob_is_err=False).then_inc(ov["gathered"].sem, 16)
                        pool.wait_ge(ov["result"].sem, ov["result"].base + n + 1 + e)
                        bump(pool)
                        pool.indirect_dma_start(out=moe_sum, out_offset=bass.IndirectOffsetOnAxis(ap=list_idx[:, 0:1], axis=0), in_=y[0][:, :], in_offset=None,
                                                       bounds_check=T - 1, oob_is_err=False, compute_op=ALU.add).then_inc(ov["added"].sem, 16)
                        pool.wait_ge(ov["added"].sem, ov["added"].base + 16 * (n + 1) + 16 * e)
                        pool.sem_inc(ov["free"].sem, 1)
                    over_passes(pool, lambda: None, expert)
            mo.close()
            if layer == 0:
                nonlocal w_dkv
                w_dkv = sb("w_dkv", [P, KD, KV_LORA + D_ROPE], scope=ln)

            with nc.Block(name=f"moe_norm{layer}") as block:
                @block.sync
                def _(sp):
                    for tt in range(TT):
                        sp.dma_start(resid[:, tt, :], moe_sum[tt * P:(tt + 1) * P, :]).then_inc(x_in[tt].sem, 16)
                    if layer == 0:
                        sp.dma_start(w_dkv[:, :, :], rows_pk(a["kv_w_dkv"], 0, KV_LORA + D_ROPE)).then_inc(mla_in.sem, 16)
                        load_units(sp, nxt[0], nxt[0] + RING)
                        nxt[0] += RING
                    else:
                        for tt in range(TT):
                            sp.wait_ge(ln_done.sem, ln_done.base + tt + 1)
                            sp.dma_start(out[0, tt * P:(tt + 1) * P, :], resid[:, tt, :]).then_inc(out_stored.sem, 16)
                        sp.wait_ge(out_stored.sem, out_stored.base + 16 * TT)

                if layer == 0:
                    @block.tensor
                    def _(pe):
                        pe_transpose_tokens(pe, resid_block, lambda tt, half: pe.wait_ge(ln_done.sem, ln_done.base + tt + 1))

                @block.scalar
                def _(act):
                    for tt in range(TT):
                        act_layer_norm(act, tt, stats)
                        if layer == 0 and tt >= 1:
                            act_copy_transposed(act, tt - 1)
                    if layer == 0:
                        act_copy_transposed(act, TT - 1)

                @block.vector
                def _(v):
                    v.wait_ge(small_in.sem, small_in.base + 32)
                    for tt in range(TT):
                        v.wait_ge(x_in[tt].sem, 16 * (layer + 2))
                        dve_layer_norm(v, tt, stats, gain, bias)
            small_in.base += 32
            for c in (ln_done, var_ready, std_ready):
                c.base += TT
            if layer == 1:
                ln.close()

        out_stored = sem("out_stored")
        mla_in = sem("mla_in")
        ln2 = [ExitStack(), ExitStack()]
        w_dkv = None
        moe(0)
        att = ExitStack()
        kT = sb("kT", [P, H, T], scope=att)
        k_ropeT = sb("k_ropeT", [P, T], scope=att)
        v_all = sb("v_all", [P, TT, D], scope=att)
        qT = sb("qT", [P, H, T], scope=att)
        q_ropeT = sb("q_ropeT", [P, H // 2, T], scope=att)

        mla = ExitStack()
        kv_norm_w = sb("kv_norm_w", [P, KV_LORA], scope=mla)
        q_norm_w = sb("q_norm_w", [P, Q_LORA], scope=mla)
        rope = sb("rope", [P, 2, TT, RH], scope=mla)
        ckv = sb("ckv", [P, TT, KV_LORA + D_ROPE], scope=mla)
        k_rope2 = sb("k_rope2", [P, TT, 2, D_ROPE], scope=mla)
        cq = sb("cq", [P, TT, Q_LORA], scope=mla)
        low_sq = sb("low_sq", [P, Q_LORA], scope=mla)
        low_ms = sb("low_ms", [P, 2, TT], scope=mla)
        cT = sb("cT", [P, KC, T], scope=mla)
        cqT = sb("cqT", [P, KQ, T], scope=mla)
        rot = sb("rot", [P, TT, 2, D_ROPE], scope=mla)
        rot_tmp = sb("rot_tmp", [P, TT, 2, D_ROPE], scope=mla)
        ckv_ready = sem("ckv_ready")
        ckv_copied = sem("ckv_copied")
        cq_copied = sem("cq_copied")
        ms_done = sem("ms_done")
        root_done = sem("root_done")
        kv_normed = sem("kv_normed")
        q_normed = sem("q_normed")
        low_ready = sem("low_ready")
        low_copied = sem("low_copied")
        ukv_copied = sem("ukv_copied")
        uq_copied = sem("uq_copied")
        rotated = sem("rotated")
        rotT_ready = sem("rotT_ready")
        rotT_copied = sem("rotT_copied")

        def rotated_T(pe, j):
            pe.wait_ge(rotated.sem, rotated.base + j + 1)
            if j >= 2:
                pe.wait_ge(rotT_copied.sem, rotT_copied.base + j - 1)
            for tt in range(TT):
                last = nc.tensor.transpose(bank[6 + j % 2][:, tt * P:(tt + 1) * P], rot[:, tt, :, :].rearrange("p a d -> p (a d)"), ident)
            last.then_inc(rotT_ready.sem, 1)

        def copy_rotated(act, j):
            act.wait_ge(rotT_ready.sem, rotT_ready.base + j + 1)
            nc.scalar.copy(q_ropeT[:, j, :], bank[6 + j % 2][:, :]).then_inc(rotT_copied.sem, 1)

        with nc.Block(name="mla_projections") as block:
            @block.sync
            def _(sp):
                sp.dma_start(rope[:, :, :, :], a["rope"].rearrange("p (c t r) -> p c t r", c=2, t=TT)).then_inc(mla_in.sem, 16)
                sp.dma_start(kv_norm_w[:, :], a["kv_norm_w"].partition_broadcast(P)).then_inc(mla_in.sem, 16)
                sp.dma_start(q_norm_w[:, :], a["b_qnorm_w"][0].partition_broadcast(P)).then_inc(mla_in.sem, 16)
                load_units(sp, nxt[0], UNIT_OUT[1] + 4)
                nxt[0] = UNIT_OUT[1] + 4

            @block.tensor
            def _(pe):
                pe.wait_ge(tr_copied.sem, tr_copied.base + 2 * TT)
                pe.wait_ge(mla_in.sem, mla_in.base + 64)
                for tt in range(TT):
                    if tt >= 2:
                        pe.wait_ge(ckv_copied.sem, ckv_copied.base + tt - 1)
                    for k in range(KD):
                        last = nc.tensor.matmul(bank[4 + tt % 2][:, 0:KV_LORA + D_ROPE], lhsT=hT[:, k, tt * P:(tt + 1) * P], rhs=w_dkv[:, k, :], start=k == 0, stop=k == KD - 1)
                    last.then_inc(ckv_ready.sem, 1)
                for n in range(2 * TT):
                    u, tt = divmod(n, TT)
                    if tt == 0:
                        unit_wait(pe, UNIT_DQ + u)
                    if n < 2:
                        pe.wait_ge(ckv_copied.sem, ckv_copied.base + TT - 1 + n)
                    else:
                        pe.wait_ge(cq_copied.sem, cq_copied.base + n - 1)
                    w = unit_cols(UNIT_DQ + u)
                    for k in range(KD):
                        last = nc.tensor.matmul(bank[4 + n % 2][:, 0:256], lhsT=hT[:, k, tt * P:(tt + 1) * P], rhs=w[:, k, :], start=k == 0, stop=k == KD - 1)
                    last.then_inc(cq_ready.sem, 1)
                for tt in range(TT):
                    pe.wait_ge(kv_normed.sem, kv_normed.base + tt + 1)
                    if tt >= 2:
                        pe.wait_ge(low_copied.sem, low_copied.base + tt - 1)
                    for j in range(KC):
                        nc.tensor.transpose(bank[tt % 2][:, j * P:(j + 1) * P], ckv[:, tt, j * P:(j + 1) * P], ident)
                    nc.tensor.transpose(bank[tt % 2][:, KC * P:(KC + 1) * P], k_rope2[:, tt, :, :].rearrange("p a d -> p (a d)"), ident).then_inc(low_ready.sem, 1)
                pe.wait_ge(low_copied.sem, low_copied.base + TT)
                for j in range(2):
                    unit_wait(pe, UNIT_UKV + j)
                    w = unit_cols(UNIT_UKV + j)
                    for m in range(8):
                        n = 8 * j + m
                        if n < 2:
                            pe.wait_ge(cq_copied.sem, cq_copied.base + 2 * TT - 1 + n)
                        else:
                            pe.wait_ge(ukv_copied.sem, ukv_copied.base + n - 1)
                        for k in range(KC):
                            if m < HG:
                                last = nc.tensor.matmul(bank[4 + n % 2][:, :], lhsT=w[:, k, m * 256:m * 256 + P], rhs=cT[:, k, :], start=k == 0, stop=k == KC - 1)
                            else:
                                tt = m - HG
                                values = w[:, k, :].rearrange("p (h c) -> p h c", c=256)[:, :, P:256]
                                last = nc.tensor.matmul(bank[4 + n % 2][:, :], lhsT=cT[:, k, tt * P:(tt + 1) * P], rhs=values, start=k == 0, stop=k == KC - 1)
                        last.then_inc(ukv_ready.sem, 1)
                for tt in range(TT):
                    pe.wait_ge(q_normed.sem, q_normed.base + tt + 1)
                    pe.wait_ge(low_copied.sem, low_copied.base + TT + tt - 1)
                    for j in range(KQ):
                        last = nc.tensor.transpose(bank[tt % 2][:, j * P:(j + 1) * P], cq[:, tt, j * P:(j + 1) * P], ident)
                    last.then_inc(low_ready.sem, 1)
                pe.wait_ge(low_copied.sem, low_copied.base + 2 * TT)
                for j in range(4):
                    unit_wait(pe, UNIT_UQ + j)
                    w = unit_cols(UNIT_UQ + j)
                    for m in range(3):
                        n = 3 * j + m
                        if n < 2:
                            pe.wait_ge(ukv_copied.sem, ukv_copied.base + 15 + n)
                        else:
                            pe.wait_ge(uq_copied.sem, uq_copied.base + n - 1)
                        b = bank[4 + n % 2]
                        if m < 2:
                            for k in range(KQ):
                                last = nc.tensor.matmul(b[:, :], lhsT=w[:, k, m * QH:m * QH + P], rhs=cqT[:, k, :], start=k == 0, stop=k == KQ - 1)
                        else:
                            for tt in range(TT):
                                for k in range(KQ):
                                    turn = w[:, k, :].rearrange("p (h c) -> p h c", c=QH)[:, :, P:QH]
                                    last = nc.tensor.matmul(b[:, tt * P:(tt + 1) * P], lhsT=cqT[:, k, tt * P:(tt + 1) * P], rhs=turn, start=k == 0, stop=k == KQ - 1)
                        last.then_inc(uq_ready.sem, 1)
                    if j >= 1:
                        rotated_T(pe, j - 1)
                rotated_T(pe, 3)

            @block.scalar
            def _(act):
                for tt in range(TT):
                    act.wait_ge(ckv_ready.sem, ckv_ready.base + tt + 1)
                    nc.scalar.copy(ckv[:, tt, :], bank[4 + tt % 2][:, 0:KV_LORA + D_ROPE]).then_inc(ckv_copied.sem, 1)
                for n in range(2 * TT):
                    u, tt = divmod(n, TT)
                    act.wait_ge(cq_ready.sem, cq_ready.base + n + 1)
                    nc.scalar.copy(cq[:, tt, u * 256:(u + 1) * 256], bank[4 + n % 2][:, 0:256]).then_inc(cq_copied.sem, 1)
                    if n == 2:
                        act.wait_ge(ms_done.sem, ms_done.base + TT)
                        nc.scalar.activation(low_ms[:, 0, :], low_ms[:, 0, :], ACT.Sqrt, bias=eps_col[:, 0:1], scale=1.0 / KV_LORA).then_inc(root_done.sem, 1)
                act.wait_ge(ms_done.sem, ms_done.base + 2 * TT)
                nc.scalar.activation(low_ms[:, 1, :], low_ms[:, 1, :], ACT.Sqrt, bias=eps_col[:, 0:1], scale=1.0 / Q_LORA).then_inc(root_done.sem, 1)
                for tt in range(TT):
                    act.wait_ge(low_ready.sem, low_ready.base + tt + 1)
                    nc.scalar.copy(cT[:, :, tt * P:(tt + 1) * P], heads(bank[tt % 2][:, 0:KC * P]))
                    nc.scalar.copy(k_ropeT[:, tt * P:(tt + 1) * P], bank[tt % 2][:, KC * P:(KC + 1) * P]).then_inc(low_copied.sem, 1)
                for n in range(16):
                    j, m = divmod(n, 8)
                    act.wait_ge(ukv_ready.sem, ukv_ready.base + n + 1)
                    dst = kT[:, HG * j + m, :] if m < HG else v_all[:, m - HG, j * 512:(j + 1) * 512]
                    nc.scalar.copy(dst, bank[4 + n % 2][:, :]).then_inc(ukv_copied.sem, 1)
                for tt in range(TT):
                    act.wait_ge(low_ready.sem, low_ready.base + TT + tt + 1)
                    nc.scalar.copy(cqT[:, :, tt * P:(tt + 1) * P], heads(bank[tt % 2][:, :])).then_inc(low_copied.sem, 1)
                for j in range(4):
                    for m in range(2):
                        act.wait_ge(uq_ready.sem, uq_ready.base + 3 * j + m + 1)
                        if j >= 1 or m >= 1:
                            act.wait_ge(uq_copied.sem, uq_copied.base + 3 * j + m)
                        nc.scalar.copy(qT[:, 2 * j + m, :], bank[4 + (3 * j + m) % 2][:, :]).then_inc(uq_copied.sem, 1)
                    if j >= 1:
                        copy_rotated(act, j - 1)
                copy_rotated(act, 3)

            @block.vector
            def _(v):
                def rotate(out1, out2, x1, x2, cos, sin, tmp1, tmp2, done):
                    tt_ = nc.vector.tensor_tensor
                    tt_(out1, x1, cos, ALU.mult)
                    tt_(tmp1, x2, sin, ALU.mult)
                    tt_(out2, x2, cos, ALU.mult)
                    ins = tt_(tmp2, x1, sin, ALU.mult)
                    done(ins)
                    tt_(out1, out1, tmp1, ALU.subtract)
                    return tt_(out2, out2, tmp2, ALU.add)

                for tt in range(TT):
                    v.wait_ge(ckv_copied.sem, ckv_copied.base + tt + 1)
                    link(v, "dve", nc.vector.tensor_tensor(low_sq[:, 0:KV_LORA], ckv[:, tt, 0:KV_LORA], ckv[:, tt, 0:KV_LORA], ALU.mult))
                    nc.vector.tensor_reduce(low_ms[:, 0, tt:tt + 1], low_sq[:, 0:KV_LORA], AX.X, ALU.add).then_inc(ms_done.sem, 1)
                    v.wait_ge(ms_done.sem, ms_done.base + tt + 1)
                v.wait_ge(mla_in.sem, mla_in.base + 64)
                cos, sin = rope[:, 0, :, :], rope[:, 1, :, :]
                x1, x2 = ckv[:, :, KV_LORA:KV_LORA + RH], ckv[:, :, KV_LORA + RH:]
                last = rotate(k_rope2[:, :, 0, 0:RH], k_rope2[:, :, 0, RH:], x1, x2, cos, sin, rot_tmp[:, :, 0, 0:RH], rot_tmp[:, :, 0, RH:], lambda ins: link(v, "dve", ins))
                link(v, "dve", last)
                link(v, "dve", nc.vector.tensor_copy(k_rope2[:, :, 1, :], k_rope2[:, :, 0, :]))
                v.wait_ge(root_done.sem, root_done.base + 1)
                link(v, "dve", nc.vector.reciprocal(low_ms[:, 0, :], low_ms[:, 0, :]))
                for tt in range(TT):
                    c = ckv[:, tt, 0:KV_LORA]
                    nc.vector.scalar_tensor_tensor(out=c, in0=c, scalar=low_ms[:, 0, tt:tt + 1], in1=kv_norm_w[:, :], op0=ALU.mult, op1=ALU.mult).then_inc(kv_normed.sem, 1)
                for tt in range(TT):
                    v.wait_ge(cq_copied.sem, cq_copied.base + TT + tt + 1)
                    link(v, "dve", nc.vector.tensor_tensor(low_sq[:, :], cq[:, tt, :], cq[:, tt, :], ALU.mult))
                    nc.vector.tensor_reduce(low_ms[:, 1, tt:tt + 1], low_sq[:, :], AX.X, ALU.add).then_inc(ms_done.sem, 1)
                    v.wait_ge(ms_done.sem, ms_done.base + TT + tt + 1)
                v.wait_ge(root_done.sem, root_done.base + 2)
                link(v, "dve", nc.vector.reciprocal(low_ms[:, 1, :], low_ms[:, 1, :]))
                for tt in range(TT):
                    c = cq[:, tt, :]
                    nc.vector.scalar_tensor_tensor(out=c, in0=c, scalar=low_ms[:, 1, tt:tt + 1], in1=q_norm_w[:, :], op0=ALU.mult, op1=ALU.mult).then_inc(q_normed.sem, 1)
                for j in range(4):
                    n = 3 * j + 2
                    v.wait_ge(uq_ready.sem, uq_ready.base + n + 1)
                    v.wait_ge(uq_copied.sem, uq_copied.base + n)
                    if j >= 1:
                        v.wait_ge(rotT_ready.sem, rotT_ready.base + j)
                    b = bank[4 + n % 2][:, :].rearrange("p (t a d) -> p t a d", t=TT, a=2)
                    for side in range(2):
                        def count(ins, side=side):
                            if side:
                                ins.then_inc(uq_copied.sem, 1)
                                v.wait_ge(uq_copied.sem, uq_copied.base + n + 1)
                            else:
                                link(v, "dve", ins)
                        last = rotate(rot[:, :, side, 0:RH], rot[:, :, side, RH:], b[:, :, side, 0:RH], b[:, :, side, RH:], cos, sin,
                                      rot_tmp[:, :, side, 0:RH], rot_tmp[:, :, side, RH:], count)
                    last.then_inc(rotated.sem, 1)
        for c, n in ((tr_ready, 2 * TT), (tr_copied, 2 * TT)):
            c.base += n
        mla.close()

        probs = sb("probs", [P, 3, T], scope=att)
        probsT = sb("probsT", [P, 2, TT, P], scope=att)
        peak = sb("peak", [P, 3], scope=att)
        total = sb("total", [P, 3], scope=att)
        attended = sb("attended", [P, H, T], scope=att)
        s_ready = sem("s_ready")
        s_masked = sem("s_masked")
        peak_done = sem("peak_done")
        exp_done = sem("exp_done")
        p_done = sem("p_done")
        pT_ready = sem("pT_ready")
        pT_copied = sem("pT_copied")
        pv_ready = sem("pv_ready")
        pv_copied = sem("pv_copied")
        NA = TT * H
        s_bank = (bank[0], bank[1], bank[6])

        with nc.Block(name="mla_attention") as block:
            @block.tensor
            def _(pe):
                def attend(n):
                    qt, h = divmod(n, H)
                    pe.wait_ge(pT_copied.sem, pT_copied.base + n + 1)
                    if n >= 2:
                        pe.wait_ge(pv_copied.sem, pv_copied.base + n - 1)
                    for kt in range(qt + 1):
                        last = nc.tensor.matmul(bank[4 + n % 2][:, 0:P], lhsT=v_all[:, kt, h * P:(h + 1) * P], rhs=probsT[:, n % 2, kt, :], start=kt == 0, stop=kt == qt)
                    last.then_inc(pv_ready.sem, 1)

                def transpose_probs(n):
                    qt, h = divmod(n, H)
                    pe.wait_ge(p_done.sem, p_done.base + n + 1)
                    if n >= 2:
                        pe.wait_ge(pT_copied.sem, pT_copied.base + n - 1)
                    for kt in range(qt + 1):
                        last = nc.tensor.transpose(bank[2 + n % 2][:, kt * P:(kt + 1) * P], probs[:, n % 3, kt * P:(kt + 1) * P], ident)
                    last.then_inc(pT_ready.sem, 1)

                for n in range(NA + 3):
                    if n < NA:
                        qt, h = divmod(n, H)
                        if n >= 3:
                            pe.wait_ge(exp_done.sem, exp_done.base + n - 2)
                        width, q = (qt + 1) * P, slice(qt * P, (qt + 1) * P)
                        half = slice(64 * (h % 2), 64 * (h % 2) + 64)
                        nc.tensor.matmul(s_bank[n % 3][:, 0:width], lhsT=qT[:, h, q], rhs=kT[:, h, 0:width], start=True, stop=False)
                        nc.tensor.matmul(s_bank[n % 3][:, 0:width], lhsT=q_ropeT[half, h // 2, q], rhs=k_ropeT[half, 0:width], start=False, stop=True).then_inc(s_ready.sem, 1)
                    if 2 <= n < NA + 2:
                        transpose_probs(n - 2)
                    if n >= 3:
                        attend(n - 3)

            @block.vector
            def _(v):
                for n in range(NA + 1):
                    if n < NA:
                        qt, h = divmod(n, H)
                        width = (qt + 1) * P
                        b = s_bank[n % 3]
                        v.wait_ge(s_ready.sem, s_ready.base + n + 1)
                        nc.vector.tensor_tensor(b[:, qt * P:width], b[:, qt * P:width], plane(C_CAUSAL), ALU.add).then_inc(s_masked.sem, 1)
                        v.wait_ge(s_masked.sem, s_masked.base + n + 1)
                        if n >= 3:
                            v.wait_ge(exp_done.sem, exp_done.base + n - 2)
                        link(v, "dve", nc.vector.reduce_max(peak[:, n % 3:n % 3 + 1], b[:, 0:width], AX.X))
                        nc.vector.tensor_single_scalar(peak[:, n % 3:n % 3 + 1], peak[:, n % 3:n % 3 + 1], -ATT_SCALE, ALU.mult).then_inc(peak_done.sem, 1)
                    if n >= 1:
                        m = n - 1
                        width = (m // H + 1) * P
                        v.wait_ge(exp_done.sem, exp_done.base + m + 1)
                        t = total[:, m % 3:m % 3 + 1]
                        link(v, "dve", nc.vector.reciprocal(t, t))
                        nc.vector.tensor_scalar(probs[:, m % 3, 0:width], probs[:, m % 3, 0:width], t, None, ALU.mult).then_inc(p_done.sem, 1)

            @block.scalar
            def _(act):
                def copy_probs(n):
                    qt = n // H
                    act.wait_ge(pT_ready.sem, pT_ready.base + n + 1)
                    if n >= 2:
                        act.wait_ge(pv_ready.sem, pv_ready.base + n - 1)
                    nc.scalar.copy(probsT[:, n % 2, 0:qt + 1, :], heads(bank[2 + n % 2][:, 0:(qt + 1) * P])).then_inc(pT_copied.sem, 1)

                def copy_out(n):
                    qt, h = divmod(n, H)
                    act.wait_ge(pv_ready.sem, pv_ready.base + n + 1)
                    nc.scalar.copy(attended[:, h, qt * P:(qt + 1) * P], bank[4 + n % 2][:, 0:P]).then_inc(pv_copied.sem, 1)

                for n in range(NA + 3):
                    if n < NA:
                        width = (n // H + 1) * P
                        act.wait_ge(peak_done.sem, peak_done.base + n + 1)
                        if n >= 3:
                            act.wait_ge(pT_ready.sem, pT_ready.base + n - 2)
                            act.wait_ge(p_done.sem, p_done.base + n - 2)
                        nc.scalar.activation(probs[:, n % 3, 0:width], s_bank[n % 3][:, 0:width], ACT.Exp, bias=peak[:, n % 3:n % 3 + 1], scale=ATT_SCALE,
                                                 accum_out=total[:, n % 3:n % 3 + 1]).then_inc(exp_done.sem, 1)
                    if 2 <= n < NA + 2:
                        copy_probs(n - 2)
                    if n >= 3:
                        copy_out(n - 3)

        nothing = lambda *_: None
        mixer_out("mla_out", 1, attended, {"pe": nothing, "dve": nothing, "act": nothing, "act_copy": nothing, "pe_copied": nothing})
        att.close()
        ln2[0].close()
        moe(1)


def kernel(**inputs):
    import concourse.bacc as bacc
    from concourse.bass_utils import run_bass_kernel_spmd

    nc = bacc.Bacc("TRN2", target_bir_lowering=False, num_devices=1)
    table, rope = constants()
    arrays = {name: np.ascontiguousarray(value) for name, value in inputs.items()}
    arrays["const"], arrays["rope"] = table, rope
    a = {name: nc.dram_tensor(f"in_{name}", v.shape, mybir.dt.from_np(v.dtype), kind="ExternalInput").ap() for name, v in arrays.items()}
    out = nc.dram_tensor("out", (1, T, D), F32, kind="ExternalOutput").ap()
    build(nc, a, out)
    r = run_bass_kernel_spmd(nc, [{f"in_{name}": v for name, v in arrays.items()}], core_ids=[0])
    return r.results[0]["out"]
```
